# Optimizing a Trainium2 kernel written in Bass

```python
import jax, jax.numpy as jnp
from jax import lax
import numpy as np

D_MODEL = 1024
BATCH = 1
SEQ = 512
DEPTH = 1

HEAD_DIM = 64
RWKV_HEADS = 16
RWKV_DIM = RWKV_HEADS * HEAD_DIM
DECAY_LORA = 64
AAA_LORA = 64
GATE_LORA = 160
GN_EPS = HEAD_DIM * 1e-5
RWKV_IN = 3 * RWKV_DIM + DECAY_LORA + AAA_LORA + GATE_LORA
DIL_GROUPS = ((128, 1), (512, 4), (2048, 16))
HEADS_PER_GROUP = 4
ATTN_HEADS = 3 * HEADS_PER_GROUP
ATTN_DIM = ATTN_HEADS * HEAD_DIM
ATTN_OUT_DIM = HEADS_PER_GROUP * HEAD_DIM
IN_SPLITS = (RWKV_DIM, RWKV_DIM, RWKV_DIM, DECAY_LORA, AAA_LORA, GATE_LORA,
             ATTN_DIM, ATTN_DIM, ATTN_DIM, D_MODEL, D_MODEL)
N_IN = RWKV_IN + 3 * ATTN_DIM + 2 * D_MODEL
MEM_LEN = 256
XATTN_HEADS = 4
XATTN_HEAD_DIM = D_MODEL // XATTN_HEADS
FFN_DIM = 4 * D_MODEL
NORM_EPS = 1e-6


def rmsnorm(x, g):
    xf = x.astype(jnp.float32)
    y = xf * lax.rsqrt(jnp.mean(xf * xf, axis=-1, keepdims=True) + NORM_EPS) * g.astype(jnp.float32)
    return y.astype(x.dtype)

def alibi_slopes(n_heads):
    return jnp.exp2(-8.0 * (jnp.arange(n_heads, dtype=jnp.float32) + 1.0) / n_heads)

def rwkv7_scan(r, w, k, v, a_, b_):
    B, S, H, N = r.shape

    def step(state, inp):
        r_t, w_t, k_t, v_t, a_t, b_t = inp
        sa = jnp.einsum('bhij,bhj->bhi', state, a_t)
        state = state * w_t[:, :, None, :] + sa[..., None] * b_t[:, :, None, :] + v_t[..., None] * k_t[:, :, None, :]
        return state, jnp.einsum('bhij,bhj->bhi', state, r_t)

    xs = tuple(jnp.moveaxis(t, 1, 0) for t in (r, w, k, v, a_, b_))
    _, ys = lax.scan(step, jnp.zeros((B, H, N, N), jnp.float32), xs)
    return jnp.moveaxis(ys, 0, 1)

def rwkv7_mix(p_r, p_k, p_v, p_wd, p_ad, p_gd, w0, w2, a0, a2, g2, k_k, k_a, r_k, gn_w, gn_b):
    B, S, _ = p_r.shape
    heads = lambda t: t.reshape(B, S, RWKV_HEADS, HEAD_DIM)
    w_log = -jax.nn.softplus(-(w0 + jnp.tanh(p_wd) @ w2)) - 0.5
    decay = jnp.exp(-jnp.exp(w_log))
    a = jax.nn.sigmoid(a0 + p_ad @ a2)
    g = jax.nn.sigmoid(p_gd) @ g2
    kk = heads(p_k * k_k)
    kk = kk / jnp.maximum(jnp.sqrt(jnp.sum(kk * kk, axis=-1, keepdims=True)), 1e-12)
    k = p_k * (1.0 + (a - 1.0) * k_a)
    r, k, v, decay, a = heads(p_r), heads(k), heads(p_v), heads(decay), heads(a)
    y = rwkv7_scan(r, decay, k, v, -kk, kk * a)
    mean = jnp.mean(y, axis=-1, keepdims=True)
    var = jnp.mean(jnp.square(y - mean), axis=-1, keepdims=True)
    yn = ((y - mean) * lax.rsqrt(var + GN_EPS)).reshape(B, S, RWKV_DIM) * gn_w + gn_b
    bonus = (jnp.sum(r * k * r_k, axis=-1, keepdims=True) * v).reshape(B, S, RWKV_DIM)
    return (yn + bonus) * g

def dilated_attention(q, k, v, window, dilation, slopes):
    B, S, H, Dh = q.shape
    blk = window // dilation
    span = blk * dilation
    Sp = -(-S // span) * span
    nb = Sp // span
    padw = ((0, 0), (0, Sp - S), (0, 0), (0, 0))

    def blocks(t):
        return jnp.pad(t, padw).astype(jnp.float32).reshape(B, nb, blk, dilation, H, Dh)

    def with_prev(t):
        prev = jnp.pad(t, ((0, 0), (1, 0), (0, 0), (0, 0), (0, 0), (0, 0)))[:, :-1]
        return jnp.concatenate([prev, t], axis=2)

    qb = blocks(q) * (Dh ** -0.5)
    kc, vc = with_prev(blocks(k)), with_prev(blocks(v))
    s = jnp.einsum('bnqrhc,bnkrhc->bnrhqk', qb, kc)
    qi = jnp.arange(blk)[:, None]
    ki = jnp.arange(2 * blk)[None, :]
    steps = qi + blk - ki
    in_band = (steps >= 0) & (steps <= blk)
    exists = (jnp.arange(nb)[:, None, None] > 0) | (ki >= blk)[None]
    valid = in_band[None] & exists
    bias = -slopes[:, None, None] * (steps * dilation).astype(jnp.float32)[None]
    s = jnp.where(valid[None, :, None, None], s + bias[None, None, None], -jnp.inf)
    lse = jax.nn.logsumexp(s, axis=-1)
    p = jnp.exp(s - lse[..., None])
    o = jnp.einsum('bnrhqk,bnkrhc->bnqrhc', p, vc).reshape(B, Sp, H, Dh)[:, :S]
    lse = jnp.transpose(lse, (0, 1, 4, 2, 3)).reshape(B, Sp, H)[:, :S]
    return o, lse

def dilated_mixture(q, k, v):
    B, S = q.shape[:2]
    slopes = alibi_slopes(ATTN_HEADS)
    outs, lses = [], []
    for gi, (window, dilation) in enumerate(DIL_GROUPS):
        hs = slice(gi * HEADS_PER_GROUP, (gi + 1) * HEADS_PER_GROUP)
        o, l = dilated_attention(q[:, :, hs], k[:, :, hs], v[:, :, hs], window, dilation, slopes[hs])
        outs.append(o)
        lses.append(l)
    wts = jax.nn.softmax(jnp.stack(lses, axis=0), axis=0)
    y = jnp.sum(wts[..., None] * jnp.stack(outs, axis=0), axis=0)
    return y.reshape(B, S, ATTN_OUT_DIM)

def memory_cross_attention(xn, memn, wq, w_kv, wo):
    B, S, _ = xn.shape
    q = (xn @ wq).astype(jnp.float32).reshape(B, S, XATTN_HEADS, XATTN_HEAD_DIM)
    kv = (memn @ w_kv).astype(jnp.float32).reshape(B, MEM_LEN, 2, XATTN_HEADS, XATTN_HEAD_DIM)
    s = jnp.einsum('bshc,bmhc->bhsm', q, kv[:, :, 0]) * (XATTN_HEAD_DIM ** -0.5)
    p = jax.nn.softmax(s, axis=-1)
    o = jnp.einsum('bhsm,bmhc->bshc', p, kv[:, :, 1]).reshape(B, S, D_MODEL)
    return (o @ wo.astype(jnp.float32)).astype(xn.dtype)

def first_inputs(seed: int = 0) -> dict:
    key = jax.random.key(seed)
    ks = jax.random.split(key, 32)
    f32 = jnp.float32
    nrm = lambda k, shape, scale: jax.random.normal(k, shape, f32) * scale
    L = DEPTH
    return {
        'x': jax.random.normal(ks[0], (BATCH, SEQ, D_MODEL), f32),
        'mem': jax.random.normal(ks[1], (BATCH, MEM_LEN, D_MODEL), f32),
        'norm_mix_g': 1.0 + nrm(ks[2], (L, D_MODEL), 0.02),
        'w_in': nrm(ks[3], (L, D_MODEL, N_IN), D_MODEL ** -0.5),
        'shift_mu': jax.random.uniform(ks[4], (L, RWKV_IN), f32),
        'w0': jax.random.uniform(ks[5], (L, RWKV_DIM), f32, -5.0, 1.0),
        'w2': nrm(ks[6], (L, DECAY_LORA, RWKV_DIM), 0.1),
        'a0': nrm(ks[7], (L, RWKV_DIM), 0.1),
        'a2': nrm(ks[8], (L, AAA_LORA, RWKV_DIM), 0.1),
        'g2': nrm(ks[9], (L, GATE_LORA, RWKV_DIM), GATE_LORA ** -0.5),
        'k_k': 0.85 + nrm(ks[10], (L, RWKV_DIM), 0.05),
        'k_a': 1.0 + nrm(ks[11], (L, RWKV_DIM), 0.05),
        'r_k': nrm(ks[12], (L, RWKV_HEADS, HEAD_DIM), 0.1),
        'gn_w': 1.0 + nrm(ks[13], (L, RWKV_DIM), 0.02),
        'gn_b': nrm(ks[14], (L, RWKV_DIM), 0.02),
        'p_rwkv': nrm(ks[15], (L, RWKV_DIM, D_MODEL), RWKV_DIM ** -0.5),
        'p_attn': nrm(ks[16], (L, ATTN_OUT_DIM, D_MODEL), ATTN_OUT_DIM ** -0.5),
        'w_out': nrm(ks[17], (L, D_MODEL, D_MODEL), D_MODEL ** -0.5),
        'norm_x_g': 1.0 + nrm(ks[18], (L, D_MODEL), 0.02),
        'norm_mem_g': 1.0 + nrm(ks[19], (L, D_MODEL), 0.02),
        'xa_wq': nrm(ks[20], (L, D_MODEL, D_MODEL), D_MODEL ** -0.5),
        'xa_wkv': nrm(ks[21], (L, D_MODEL, 2 * D_MODEL), D_MODEL ** -0.5),
        'xa_wo': nrm(ks[22], (L, D_MODEL, D_MODEL), D_MODEL ** -0.5),
        'norm_ffn_g': 1.0 + nrm(ks[23], (L, D_MODEL), 0.02),
        'ffn_w1': nrm(ks[24], (L, D_MODEL, FFN_DIM), D_MODEL ** -0.5),
        'ffn_w2': nrm(ks[25], (L, FFN_DIM, D_MODEL), FFN_DIM ** -0.5),
        'norm_final_g': 1.0 + nrm(ks[26], (D_MODEL,), 0.02),
    }

def first_block(x, mem, norm_mix_g, w_in, shift_mu, w0, w2, a0, a2, g2, k_k, k_a, r_k, gn_w, gn_b,
              p_rwkv, p_attn, w_out, norm_x_g, norm_mem_g, xa_wq, xa_wkv, xa_wo,
              norm_ffn_g, ffn_w1, ffn_w2, norm_final_g):
    f32 = jnp.float32
    B, S, _ = x.shape
    bounds = list(np.cumsum(IN_SPLITS)[:-1])
    h = x
    for l in range(DEPTH):
        n = rmsnorm(h, norm_mix_g[l])
        proj = (n @ w_in[l]).astype(f32)
        rw = proj[..., :RWKV_IN]
        rw_prev = jnp.pad(rw, ((0, 0), (1, 0), (0, 0)))[:, :-1]
        proj = jnp.concatenate([rw + shift_mu[l].astype(f32) * (rw_prev - rw), proj[..., RWKV_IN:]], axis=-1)
        (p_r, p_k, p_v, p_wd, p_ad, p_gd, q, k, v, gate_r, gate_a) = jnp.split(proj, bounds, axis=-1)
        y_rwkv = rwkv7_mix(p_r, p_k, p_v, p_wd, p_ad, p_gd,
                           w0[l].astype(f32), w2[l].astype(f32), a0[l].astype(f32), a2[l].astype(f32),
                           g2[l].astype(f32), k_k[l].astype(f32), k_a[l].astype(f32), r_k[l].astype(f32),
                           gn_w[l].astype(f32), gn_b[l].astype(f32))
        hd = lambda t: t.reshape(B, S, ATTN_HEADS, HEAD_DIM)
        y_attn = dilated_mixture(hd(q), hd(k), hd(v))
        merged = (jax.nn.sigmoid(gate_r) * (y_rwkv @ p_rwkv[l].astype(f32))
                  + jax.nn.sigmoid(gate_a) * (y_attn @ p_attn[l].astype(f32)))
        h = h + (merged @ w_out[l].astype(f32)).astype(h.dtype)
        h = h + memory_cross_attention(rmsnorm(h, norm_x_g[l]), rmsnorm(mem, norm_mem_g[l]),
                                       xa_wq[l], xa_wkv[l], xa_wo[l])
        u = rmsnorm(h, norm_ffn_g[l]) @ ffn_w1[l]
        h = h + (jnp.square(jax.nn.relu(u)) @ ffn_w2[l]).astype(h.dtype)
    return rmsnorm(h, norm_final_g)


DEPTH_2 = 2

F_WIDTH = D_MODEL
F_GROUP_DIM = 128
F_GROUPS = F_WIDTH // F_GROUP_DIM
RET_HEADS = 4
RET_DK = D_MODEL // RET_HEADS
RET_DV = D_MODEL // RET_HEADS
RET_QK = RET_HEADS * RET_DK
RET_V = RET_HEADS * RET_DV
CHUNK = 128
ROPE_BASE = 10000.0
DECAY_OFFSET_FWD = 0.0
DECAY_OFFSET_BWD = 0.5
D_FF = 2816
CONV_WIDTH = 3
N_MOD = 6
EPS = 1e-6
IN_SIZES = (F_WIDTH, RET_QK, RET_QK, RET_V, RET_V, D_MODEL, D_MODEL)
D_IN = F_WIDTH + 2 * RET_QK + 2 * RET_V + 2 * D_MODEL


def rmsnorm_2(x, g):
    xf = x.astype(jnp.float32)
    y = xf * lax.rsqrt(jnp.mean(xf * xf, axis=-1, keepdims=True) + EPS)
    return (y * g.astype(jnp.float32)).astype(x.dtype)

def decay_logs(offset):
    expo = -(5.0 + offset) - jnp.arange(RET_HEADS, dtype=jnp.float32)
    return jnp.log1p(-jnp.exp2(expo))

def fourier_mix(u):
    B, S, _ = u.shape
    ug = u.astype(jnp.float32).reshape(B, S, F_GROUPS, F_GROUP_DIM)
    y = jnp.fft.fft2(ug, axes=(1, 3), norm='ortho').real
    return y.reshape(B, S, F_WIDTH).astype(u.dtype)

def rotary(t):
    S = t.shape[1]
    half = t.shape[-1] // 2
    inv_freq = ROPE_BASE ** (-jnp.arange(half, dtype=jnp.float32) / half)
    ang = jnp.arange(S, dtype=jnp.float32)[:, None] * inv_freq[None, :]
    cos = jnp.cos(ang)[None, :, None, :]
    sin = jnp.sin(ang)[None, :, None, :]
    t1, t2 = t[..., :half], t[..., half:]
    return jnp.concatenate([t1 * cos - t2 * sin, t1 * sin + t2 * cos], axis=-1)

def chunk_retention(q, k, v, log_gamma, strict):
    B, H, S, dk = q.shape
    dv = v.shape[-1]
    n_chunks = S // CHUNK
    qc = q.reshape(B, H, n_chunks, CHUNK, dk)
    kc = k.reshape(B, H, n_chunks, CHUNK, dk)
    vc = v.reshape(B, H, n_chunks, CHUNK, dv)
    j = jnp.arange(CHUNK, dtype=jnp.float32)
    diff = j[:, None] - j[None, :]
    keep = (diff > 0) if strict else (diff >= 0)
    dmask = jnp.where(keep[None], jnp.exp(log_gamma[:, None, None] * jnp.maximum(diff, 0.0)[None]), 0.0)
    scores = jnp.einsum('bhncd,bhnld->bhncl', qc, kc) * dmask[None, :, None]
    intra = jnp.einsum('bhncl,bhnle->bhnce', scores, vc)
    q_decay = jnp.exp(log_gamma[:, None] * (j + 1.0))[None, :, :, None]
    k_decay = jnp.exp(log_gamma[:, None] * (CHUNK - 1.0 - j))[None, :, :, None]
    chunk_decay = jnp.exp(log_gamma * CHUNK)[None, :, None, None]

    def step(state, xs):
        qi, ki, vi = xs
        cross = jnp.einsum('bhcd,bhde->bhce', qi, state) * q_decay
        state = state * chunk_decay + jnp.einsum('bhcd,bhce->bhde', ki * k_decay, vi)
        return state, cross

    state0 = jnp.zeros((B, H, dk, dv), jnp.float32)
    xs = (jnp.moveaxis(qc, 2, 0), jnp.moveaxis(kc, 2, 0), jnp.moveaxis(vc, 2, 0))
    _, cross = lax.scan(step, state0, xs)
    out = intra + jnp.moveaxis(cross, 0, 2)
    return out.reshape(B, H, S, dv)

def retention_branch(q, k, v, g):
    B, S, _ = q.shape
    dt = q.dtype
    qh = rotary(q.astype(jnp.float32).reshape(B, S, RET_HEADS, RET_DK)) * (RET_DK ** -0.5)
    kh = rotary(k.astype(jnp.float32).reshape(B, S, RET_HEADS, RET_DK))
    vh = v.astype(jnp.float32).reshape(B, S, RET_HEADS, RET_DV)
    qh = jnp.transpose(qh, (0, 2, 1, 3))
    kh = jnp.transpose(kh, (0, 2, 1, 3))
    vh = jnp.transpose(vh, (0, 2, 1, 3))
    fwd = chunk_retention(qh, kh, vh, decay_logs(DECAY_OFFSET_FWD), strict=False)
    bwd = jnp.flip(chunk_retention(jnp.flip(qh, axis=2), jnp.flip(kh, axis=2), jnp.flip(vh, axis=2),
                                   decay_logs(DECAY_OFFSET_BWD), strict=True), axis=2)
    y = jnp.transpose(fwd + bwd, (0, 2, 1, 3))
    mu = jnp.mean(y, axis=-1, keepdims=True)
    var = jnp.mean(jnp.square(y - mu), axis=-1, keepdims=True)
    y = (y - mu) * lax.rsqrt(var + EPS)
    y = y.reshape(B, S, RET_V) * jax.nn.silu(g.astype(jnp.float32))
    return y.astype(dt)

def token_mix(h, w_in, w_fourier, w_ret, w_out):
    proj = h @ w_in
    offsets = np.cumsum(IN_SIZES)[:-1].tolist()
    u_f, q, k, v, g, a_f, a_r = jnp.split(proj, offsets, axis=-1)
    y_f = fourier_mix(u_f) @ w_fourier
    y_r = retention_branch(q, k, v, g) @ w_ret
    merged = jax.nn.sigmoid(a_f) * y_f + jax.nn.sigmoid(a_r) * y_r
    return merged @ w_out

def conv_ffn(h, w_up, conv_w, conv_b, w_down):
    S = h.shape[1]
    u = h @ w_up
    pad = CONV_WIDTH // 2
    up = jnp.pad(u, ((0, 0), (pad, pad), (0, 0)))
    u = sum(up[:, i:i + S] * conv_w[i] for i in range(CONV_WIDTH)) + conv_b
    a, b = jnp.split(u, 2, axis=-1)
    return (jax.nn.gelu(a, approximate=False) * b) @ w_down

def second_inputs(seed: int = 0) -> dict:
    key = jax.random.key(seed)
    ks = jax.random.split(key, 15)

    def nrm(k, shape, scale):
        return jax.random.normal(k, shape, jnp.float32) * scale

    return {
        'x': nrm(ks[0], (BATCH, SEQ, D_MODEL), 1.0),
        'c': nrm(ks[1], (BATCH, D_MODEL), 1.0),
        'norm1_g': 1.0 + nrm(ks[2], (DEPTH_2, D_MODEL), 0.02),
        'norm2_g': 1.0 + nrm(ks[3], (DEPTH_2, D_MODEL), 0.02),
        'ada_w': nrm(ks[4], (DEPTH_2, D_MODEL, N_MOD * D_MODEL), 0.5 * D_MODEL ** -0.5),
        'ada_b': nrm(ks[5], (DEPTH_2, N_MOD * D_MODEL), 0.02),
        'w_in': nrm(ks[6], (DEPTH_2, D_MODEL, D_IN), D_MODEL ** -0.5),
        'w_fourier': nrm(ks[7], (DEPTH_2, F_WIDTH, D_MODEL), F_WIDTH ** -0.5),
        'w_ret': nrm(ks[8], (DEPTH_2, RET_V, D_MODEL), RET_V ** -0.5),
        'w_out': nrm(ks[9], (DEPTH_2, D_MODEL, D_MODEL), D_MODEL ** -0.5),
        'ffn_up': nrm(ks[10], (DEPTH_2, D_MODEL, 2 * D_FF), D_MODEL ** -0.5),
        'conv_w': nrm(ks[11], (DEPTH_2, CONV_WIDTH, 2 * D_FF), CONV_WIDTH ** -0.5),
        'conv_b': nrm(ks[12], (DEPTH_2, 2 * D_FF), 0.02),
        'ffn_down': nrm(ks[13], (DEPTH_2, D_FF, D_MODEL), D_FF ** -0.5),
        'final_g': 1.0 + nrm(ks[14], (D_MODEL,), 0.02),
    }

def second_block(x, c, norm1_g, norm2_g, ada_w, ada_b, w_in, w_fourier, w_ret, w_out,
              ffn_up, conv_w, conv_b, ffn_down, final_g):
    c_act = jax.nn.silu(c)
    for l in range(DEPTH_2):
        mod = (c_act @ ada_w[l] + ada_b[l])[:, None, :]
        sh1, sc1, g1, sh2, sc2, g2 = jnp.split(mod, N_MOD, axis=-1)
        h = rmsnorm_2(x, norm1_g[l]) * (1.0 + sc1) + sh1
        x = x + g1 * token_mix(h, w_in[l], w_fourier[l], w_ret[l], w_out[l])
        h = rmsnorm_2(x, norm2_g[l]) * (1.0 + sc2) + sh2
        x = x + g2 * conv_ffn(h, ffn_up[l], conv_w[l], conv_b[l], ffn_down[l])
    return rmsnorm_2(x, final_g)


def setup_inputs(seed=0):
    out = dict(first_inputs(seed))
    for name, value in second_inputs(seed + 1).items():
        if name != "x":
            out[name + "_2"] = value
    return out


def reference(
    x, mem, norm_mix_g, w_in, shift_mu, w0, w2, a0, a2, g2, k_k, k_a, r_k, gn_w, gn_b, p_rwkv,
    p_attn, w_out, norm_x_g, norm_mem_g, xa_wq, xa_wkv, xa_wo, norm_ffn_g, ffn_w1, ffn_w2,
    norm_final_g, c_2, norm1_g_2, norm2_g_2, ada_w_2, ada_b_2, w_in_2, w_fourier_2, w_ret_2,
    w_out_2, ffn_up_2, conv_w_2, conv_b_2, ffn_down_2, final_g_2,
):
    x = first_block(
        x, mem, norm_mix_g, w_in, shift_mu, w0, w2, a0, a2, g2, k_k, k_a, r_k, gn_w, gn_b,
        p_rwkv, p_attn, w_out, norm_x_g, norm_mem_g, xa_wq, xa_wkv, xa_wo, norm_ffn_g, ffn_w1,
        ffn_w2, norm_final_g,
    )
    return second_block(
        x, c_2, norm1_g_2, norm2_g_2, ada_w_2, ada_b_2, w_in_2, w_fourier_2, w_ret_2, w_out_2,
        ffn_up_2, conv_w_2, conv_b_2, ffn_down_2, final_g_2,
    )


_drawn_inputs = setup_inputs


def setup_inputs(seed=0):
    import zlib

    import numpy as np

    out = dict(_drawn_inputs(seed))
    spreads = {}
    factors = {'norm_mix_g': 3.945,
     'w2': 3.452,
     'a0': 4.133,
     'k_k': 5.35,
     'k_a': 3.173,
     'gn_w': 8.0,
     'gn_b': 8.0,
     'norm_x_g': 8.0,
     'norm_mem_g': 8.0,
     'norm_ffn_g': 3.089,
     'norm1_g_2': 7.319,
     'norm2_g_2': 6.045,
     'conv_b_2': 6.457,
     'final_g_2': 2.843}
    for name, (base, spread) in spreads.items():
        noise = np.random.default_rng([zlib.crc32(name.encode()), seed]).standard_normal(out[name].shape)
        drawn = base * np.exp(spread * noise) if base else spread * noise
        out[name] = __import__('jax').numpy.asarray(drawn.astype(out[name].dtype))
    for name, factor in factors.items():
        out[name] = (out[name] * factor).astype(out[name].dtype)
    return out
```

```python
from contextlib import ExitStack

import numpy as np
import concourse.bass as bass
from concourse import mybir

P = 128
F32 = mybir.dt.float32
F32R = mybir.dt.float32r
ALU = mybir.AluOpType
ACT = mybir.ActivationFunctionType
AX_X = mybir.AxisListType.X

D = 1024
S = 512
M = 256
KT = D // P
TC = S // P
CH = 64
NC = S // CH
PAIRS = 8
AH = 12
XH = 4
FF1 = 4096 // P
FF2 = 2816 // P
LAYERS = 2
RING = 4
BANKS = 4
ARENA = 21000
UNIT = 1024
ADA = 48
EPS = 1e-6
GN_EPS = 64 * 1e-5
LOG_DECAY = -float(np.exp(-0.5))


def columns(names):
    at, out = 0, {}
    for name, n in names:
        out[name] = (at, at + n)
        at += n
    return out, at


PARAMS = [("g_mix", 8), ("mu", 27), ("w0", 8), ("a0", 8), ("k_k", 8), ("k_a", 8), ("r_k", 8), ("gn_w", 8),
          ("gn_b", 8), ("g_x", 8), ("g_mem", 8), ("g_ffn", 8), ("g_final", 8), ("c", 8), ("g_out", 8)]
for _l in range(LAYERS):
    PARAMS += [(f"norm1_{_l}", 8), (f"norm2_{_l}", 8), (f"ada_b{_l}", ADA)]
    PARAMS += [(f"conv{_i}_{_l}", 2 * FF2) for _i in range(3)] + [(f"conv_b{_l}", 2 * FF2)]
PCOL, PTOTAL = columns(PARAMS)

TABLE = [("ident", 128), ("ones", 128), ("heads", 128), ("strict", 128), ("incl", 64), ("level", 6 * 64),
         ("ident_c", 64), ("reset", 512)]
TCOL, TTOTAL = columns(TABLE)


def chunks_of(n, size=8):
    return [(a, min(size, n - a)) for a in range(0, n, size)]


class Plan:

    def __init__(self):
        self.tiles, self.stages, self.source, self.conv, self.splits = [], {}, [], [], {}

    def unit(self, *source):
        self.source.append(source)
        return len(self.source) - 1

    def plain(self, name, weight, layer, col, n, row=0, k=KT, src="A1"):
        start, per = len(self.tiles), UNIT // P
        for j in range(n):
            blocks = []
            for i in range(k):
                b = j * k + i
                if b % per == 0:
                    self.unit("blocks", weight, layer, row, col, k, b, min(per, n * k - b))
                blocks.append((len(self.source) - 1, P * (b % per), i))
            self.tiles.append(dict(blocks=blocks, src=src, rows=False))
        self.stages[name] = (start, len(self.tiles))

    def pairs(self, name, one, other, n):
        start = len(self.tiles)
        for j in range(n):
            for weight, layer, col, src in (one, other):
                u = self.unit("blocks", weight, layer, 0, col + P * j, KT, 0, KT)
                self.tiles.append(dict(blocks=[(u, P * i, i) for i in range(KT)], src=src, rows=False))
        self.stages[name] = (start, len(self.tiles))

    def token_major(self, name, weight, layer, col, cols, token_tiles, src="A1"):
        start = len(self.tiles)
        for c0 in range(0, cols, 512):
            w = min(512, cols - c0)
            per = UNIT // w
            us = [self.unit("rows", weight, layer, per * P * q, col + c0, w, per) for q in range(KT // per)]
            for t in range(token_tiles):
                self.tiles.append(dict(blocks=[(us[i // per], w * (i % per), i) for i in range(KT)], src=src,
                                       rows=True, width=w, token=t, col=c0))
        self.stages[name] = (start, len(self.tiles))

    def split(self, name, buf, n, free_after):
        self.splits[name] = (len(self.conv), len(self.conv) + n)
        for j in range(n):
            self.conv.append((buf, j, self.stages[free_after][1] if free_after else 0))


def make_plan():
    p = Plan()
    p.split("n_mix", "A1", 8, None)
    p.plain("qk", "w_in", 0, 3360, 12)
    p.token_major("v", "w_in", 0, 3360 + 1536, 768, TC)
    p.split("y_attn", "YA", 2, None)
    p.plain("lora", "w_in_lora", 0, 0, 3)
    for q in range(PAIRS):
        p.plain(f"rkv{q}", "w_in_pair", 0, 384 * q, 3)
    p.split("y_rwkv", "A2", 8, None)
    p.plain("attn_out", "p_attn", 0, 0, 8, k=2, src="YA")
    p.plain("gate_a", "w_in", 0, 3360 + 2304 + 1024, 8)
    p.pairs("rwkv_out", ("w_in", 0, 3360 + 2304, "A1"), ("p_rwkv", 0, 0, "A2"), 8)
    p.split("merged", "A1", 8, "rwkv_out")
    p.plain("mix_out", "w_out", 0, 0, 8)
    p.split("n_mem", "A2", 8, "rwkv_out")
    p.plain("mem_k", "xa_wkv", 0, 0, 8, src="A2")
    p.token_major("mem_v", "xa_wkv", 0, 1024, 1024, 2, src="A2")
    p.split("n_x", "A1", 8, "mix_out")
    p.plain("x_q", "xa_wq", 0, 0, 8)
    p.split("x_o", "A2", 8, "mem_v")
    p.plain("x_out", "xa_wo", 0, 0, 8, src="A2")
    p.split("n_ffn", "A1", 8, "x_q")
    before = "x_out"
    for c, (a, n) in enumerate(chunks_of(FF1)):
        p.plain(f"up{c}", "ffn_w1", 0, P * a, n)
        p.split(f"hidden{c}", "A2", n, before)
        p.plain(f"down{c}", "ffn_w2", 0, 0, 8, row=P * a, k=n, src="A2")
        before = f"down{c}"
    for l in range(LAYERS):
        p.split(f"n1_{l}", "A1", 8, "up3" if l == 0 else "ff_in0_2")
        p.plain(f"fourier_in{l}", "w_in_2", l, 0, 8)
        p.split(f"fourier{l}", "A2", 8, before)
        p.pairs(f"fourier_out{l}", ("w_in_2", l, 5120, "A1"), ("w_fourier_2", l, 0, "A2"), 8)
        for h in range(XH):
            p.plain(f"ret_q{l}_{h}", "w_in_2", l, 1024 + 256 * h, 2)
            p.plain(f"ret_k{l}_{h}", "w_in_2", l, 2048 + 256 * h, 2)
            p.token_major(f"ret_v{l}_{h}", "w_in_2", l, 3072 + 256 * h, 256, TC)
            p.plain(f"ret_g{l}_{h}", "w_in_2", l, 4096 + 256 * h, 2)
        p.split(f"ret{l}", "A2", 8, f"fourier_out{l}")
        p.pairs(f"ret_out{l}", ("w_in_2", l, 6144, "A1"), ("w_ret_2", l, 0, "A2"), 8)
        p.split(f"m{l}", "A1", 8, f"ret_out{l}")
        p.plain(f"out{l}", "w_out_2", l, 0, 8)
        p.split(f"n2_{l}", "A1", 8, f"out{l}")
        before = f"ret_out{l}"
        for c, (a, n) in enumerate(chunks_of(FF2)):
            p.pairs(f"ff_in{l}_{c}", ("ffn_up_2", l, P * a, "A1"), ("ffn_up_2", l, P * (FF2 + a), "A1"), n)
            p.split(f"ff{l}_{c}", "A2", n, before)
            p.plain(f"ff_out{l}_{c}", "ffn_down_2", l, 0, 8, row=P * a, k=n, src="A2")
            before = f"ff_out{l}_{c}"
    while len(p.source) % RING:
        p.unit("none")
    return p


def build_program(nc, plan, ap, out):
    tiles, stages, conv, splits = plan.tiles, plan.stages, plan.conv, plan.splits
    n_units = len(plan.source)
    last_tile = {}
    for t, T in enumerate(tiles):
        for u, _, _ in T["blocks"]:
            last_tile[u] = t

    ctx = ExitStack()
    with ctx:
        def sb(name, shape, dt=F32):
            return ctx.enter_context(nc.sbuf_tensor(name, shape, dt))

        sems = {}

        def sem(name):
            if name not in sems:
                sems[name] = ctx.enter_context(nc.semaphore(name))
            return sems[name]

        w_raw = sb("w_raw", [P, RING, UNIT])
        w_hi = sb("w_hi", [P, RING, UNIT], F32R)
        w_lo = sb("w_lo", [P, RING, UNIT], F32R)
        acts = {"A1": sb("act1", [P, 2, KT, S], F32R), "A2": sb("act2", [P, 2, KT, S], F32R),
                "YA": sb("act_attn", [P, 2, 2, S], F32R)}
        params = sb("params", [P, PTOTAL])
        table = sb("table", [P, TTOTAL])
        tmp = sb("tmp", [P, 2, S])
        squares = sb("squares", [P, 2, S])
        rstd = sb("rstd", [P, S])
        small = sb("small", [P, 4 * ADA])
        arena = sb("arena", [P, ARENA])
        banks = [ctx.enter_context(nc.psum_tensor(f"bank{i}", [P, 512], F32)) for i in range(8)]

        free_at = [0]

        def take(*shape):
            n = 1
            for x in shape:
                n *= x
            a = arena[:, free_at[0]:free_at[0] + n]
            free_at[0] += n
            assert free_at[0] <= ARENA, (free_at[0], ARENA)
            if len(shape) == 2:
                return a.rearrange("p (a b) -> p a b", b=shape[1])
            if len(shape) == 3:
                return a.rearrange("p (a b c) -> p a b c", b=shape[1], c=shape[2])
            return a

        def prm(name, j=0, n=1):
            return params[:, PCOL[name][0] + j:PCOL[name][0] + j + n]

        def tab(name):
            return table[:, TCOL[name][0]:TCOL[name][1]]

        ident, ones, heads, strict, incl, ident_c, reset = (
            tab(n) for n in ("ident", "ones", "heads", "strict", "incl", "ident_c", "reset"))
        level = tab("level").rearrange("p (l s) -> p l s", s=CH)

        H = take(KT, S)
        MERGED = take(KT, S)
        gate_buf = take(2, S)
        base = free_at[0]
        free_at[0] = KT * S
        QK = take(12, S)
        VT = take(TC, 768)
        SC = take(2, 1280)
        PT = take(1280)
        DIST = take(1280)
        att_stat = take(2, 4)
        free_at[0] = 0
        RAW = take(2, 520)
        LORA = take(S)
        GD = take(2, S)
        LW = take(4, P)
        R, K, V, SW, W, WI, WX, A_, KK, G = (take(S) for _ in range(10))
        DIFF, RK, CS = rstd[:], squares[:, 0, :], squares[:, 1, :]
        AR = take(NC, 2, CH)
        BX, KX, VX, AX, LAB, LAK, TX, TTX = (take(NC, P) for _ in range(8))
        RM = take(NC, 2, CH)
        MRK = take(NC, CH)
        VC = take(NC, CH)
        AZ = take(NC, 2, CH)
        X0C = WX.rearrange("p (c t) -> p c t", t=CH)
        NP_ = A_.rearrange("p (c t) -> p c t", t=CH)
        SC_ = CS.rearrange("p (c t) -> p c t", t=CH)
        PX, TAX, X0X, MCX, SX = AX, AX, LAK, TX, LAB
        YC, YSQ = SW, KK
        free_at[0] = base
        MEM = take(KT, M)
        KM = MERGED[:, 0:4, :].rearrange("p a (b m) -> p (a b) m", m=M)
        VM = MERGED[:, 4:8, :].rearrange("p (a b) m -> p a (b m)", a=2)
        XQ = take(KT, S)
        XP = take(TC, M)
        XPT = take(2, S)
        x_stat = take(TC, 4)
        free_at[0] = base
        ADA_W = take(4, UNIT)
        RELU = take(2, S)
        free_at[0] = base
        CS_SEQ = take(TC, S)
        SN_SEQ = take(TC, S)
        CS_FEAT = take(256)
        UF = take(2, S)
        PF = take(2, TC, 256)
        free_at[0] = base
        COS = take(S)
        SIN = take(S)
        RQ = take(2, S)
        RKY = take(2, S)
        ROT = take(4, S)
        RV = take(TC, 256)
        STRIP = take(896)
        RP = take(TC, S)
        RG = take(2, S)
        RY = take(2, S)
        free_at[0] = base
        FRAW = take(2, 528)
        CONV = take(2, 2, S)

        mods = small[:, 0:2 * ADA]
        scaled = small[:, 2 * ADA:2 * ADA + 32]
        c_act = small[:, 2 * ADA + 32:2 * ADA + 40]
        ADA_TILES = (stages["up0"][0], ADA)

        block = ctx.enter_context(nc.Block())

        def evacuated(eng, t):
            eng.wait_ge(sem(f"bank_free{t % BANKS}"), t // BANKS + 1)

        def all_evacuated(eng, stage):
            end = stages[stage][1]
            for t in range(end - BANKS, end):
                evacuated(eng, t)

        def tile_done(eng, t):
            eng.wait_ge(sem("tile_done"), t + 1)

        STEPS = [("zw", "a"), ("za", "a"), ("zg", "a"), ("ss", "v"), ("bonus", "v")]
        for h in range(2):
            STEPS += [(f"bM{h}", "v"), (f"kM{h}", "v")]
        for h in range(2):
            STEPS += [(f"tT{h}", "a"), (f"tA{h}", "a")]
        for h in range(2):
            STEPS += [(f"tB{h}", "a"), (f"tV{h}", "a")]
        for l in range(1, 6):
            for what in ("P", "D", "X"):
                for h in range(2):
                    STEPS += [(f"{what}{l}{h}", "a" if what == "X" else "v")]
            if l == 1:
                STEPS += [("tK0", "a"), ("tK1", "a"), ("Z0", "a"), ("Z1", "a")]
        STEPS += [(f"{w}{h}", "v") for w in ("TAX", "RM", "N") for h in range(2)]
        STEPS += [("scan", "v")] + [("Y", "a"), ("mean", "v"), ("var", "v")]
        INDEX = {name: n for n, (name, _) in enumerate(STEPS)}
        EVACS = {e: sum(1 for _, x in STEPS if x == e) for e in "av"}

        def emptied(eng, name, p):
            n = INDEX[name]
            e = STEPS[n][1]
            eng.wait_ge(sem("rw_emptied_" + e), p * EVACS[e] + sum(1 for _, x in STEPS[:n + 1] if x == e))

        def made(eng, name, p):
            eng.wait_ge(sem("rw_made"), p * len(STEPS) + INDEX[name] + 1)

        def rbank(name, p):
            return banks[4 + (p * len(STEPS) + INDEX[name]) % 4]

        NORMS = ["mix", "mem", "x", "ffn", "final"] + [f"{w}_{l}" for l in range(LAYERS) for w in ("n1", "n2")] + ["out"]

        def squares_before(name):
            return 8 * NORMS.index(name)

        @block.sync
        def _(sp):
            for u in range(n_units):
                k = u % RING
                if u >= RING:
                    sp.wait_ge(sem("w_low"), u - RING + 1)
                sp.dma_start(w_raw[:, k, :], ap["weights"][u]).then_inc(sem(f"w_landed{k}"), 16)
            sp.wait_ge(sem("y_done"), KT)
            sp.dma_start(out, H).then_inc(sem("stored"), 16)
            sp.wait_ge(sem("stored"), 16)

        @block.gpsimd
        def _(pool):
            n_ada = 2 * ADA
            first_ada = min(u for u, _, _ in tiles[ADA_TILES[0]]["blocks"])
            issued = 0
            for u in range(n_units):
                k = u % RING
                pool.wait_ge(sem("w_high"), u + 1)
                if u >= RING:
                    pool.wait_ge(sem("tile_done"), last_tile[u - RING] + 1)
                nc.gpsimd.tensor_tensor(w_lo[:, k, :], w_raw[:, k, :], w_hi[:, k, :].bitcast(F32),
                                        ALU.subtract).then_inc(sem("w_low"), 1)
                if u == first_ada - 2:
                    tile_done(pool, stages["x_out"][1] - 4)
                    pool.wait_ge(sem("mem_done"), 1)
                while issued < n_ada and u >= first_ada - 2 and issued < 2 * (u - first_ada + 3):
                    if issued >= 4:
                        pool.wait_ge(sem("ada_used"), issued - 3)
                    pool.dma_start(ADA_W[:, issued % 4, :], ap["ada"][issued]).then_inc(
                        sem(f"ada_landed{issued % 4}"), 16)
                    issued += 1
            assert issued == n_ada

        @block.tensor
        def _(pe):
            seen = {"low": 0, "weights": 0}

            def tile(t, first_conv, n=S):
                T = tiles[t]
                if t >= BANKS:
                    evacuated(pe, t - BANKS)
                src = acts[T["src"]]
                dst = banks[t % BANKS]
                for i, (u, col, k) in enumerate(T["blocks"]):
                    if u + 1 > seen["weights"]:
                        pe.wait_ge(sem("w_low"), u + 1)
                        seen["weights"] = u + 1
                    if first_conv + k + 1 > seen["low"]:
                        pe.wait_ge(sem("low_done"), first_conv + k + 1)
                        seen["low"] = first_conv + k + 1
                    s = u % RING
                    first, last = i == 0, i == len(T["blocks"]) - 1
                    if T["rows"]:
                        w = T["width"]
                        xs = [src[:, q, k, T["token"] * P:(T["token"] + 1) * P] for q in range(2)]
                        wh, wl = w_hi[:, s, col:col + w], w_lo[:, s, col:col + w]
                        o = dst[:, 0:w]
                        nc.tensor.matmul(o, xs[0], wh, start=first, stop=False)
                        nc.tensor.matmul(o, xs[0], wl, start=False, stop=False)
                        mm = nc.tensor.matmul(o, xs[1], wh, start=False, stop=last)
                    else:
                        wh, wl = w_hi[:, s, col:col + P], w_lo[:, s, col:col + P]
                        xh, xl = src[:, 0, k, 0:n], src[:, 1, k, 0:n]
                        o = dst[:, 0:n]
                        nc.tensor.matmul(o, wh, xh, start=first, stop=False)
                        nc.tensor.matmul(o, wh, xl, start=False, stop=False)
                        mm = nc.tensor.matmul(o, wl, xh, start=False, stop=last)
                mm.then_inc(sem("tile_done"), 1)

            def sum_squares(name, j, n=S):
                s = squares_before(name) + j
                if j == 0 and NORMS.index(name):
                    pe.wait_ge(sem("rms_ready"), NORMS.index(name))
                pe.wait_ge(sem("sq_ready"), s + 1)
                nc.tensor.matmul(banks[4][:, 0:n], ones, squares[:, s % 2, 0:n], start=(j == 0),
                                 stop=(j == KT - 1)).then_inc(sem("sq_used"), 1)

            def stage(name, split, n=S, norm=None):
                t0, t1 = stages[name]
                for t in range(t0, t1):
                    tile(t, splits[split][0], n)
                    if norm and t > t0:
                        sum_squares(norm, t - t0 - 1)
                if norm:
                    sum_squares(norm, KT - 1)

            def pair_stage(name, one, other):
                t0, t1 = stages[name]
                for t in range(t0, t1):
                    tile(t, splits[(one, other)[(t - t0) % 2]][0])

            pe.wait_ge(sem("ld_table"), 16)
            for j in range(KT):
                sum_squares("mix", j)
            stage("qk", "n_mix")
            stage("v", "n_mix")
            all_evacuated(pe, "v")

            def scores(it):
                hh, c = it // TC, it % TC
                if it >= 1:
                    pe.wait_ge(sem("att_scored"), it)
                else:
                    pe.wait_ge(sem("rms_ready"), 1)
                for g in range(3):
                    head = 4 * g + hh
                    tl, b = head // 2, 64 * (head % 2)
                    k0 = max(0, c - 1) * P if g == 0 else 0
                    mm = nc.tensor.matmul(banks[4 + g][:, 0:(c + 1) * P - k0], QK[b:b + 64, tl, c * P:(c + 1) * P],
                                          QK[b:b + 64, 6 + tl, k0:(c + 1) * P], start=True, stop=True)
                mm.then_inc(sem("att_raw"), 1)

            def att_blocks(it):
                c = it % TC
                return [(g, kc) for g in range(3) for kc in range(max(0, c - 1) if g == 0 else 0, c + 1)]

            def turn(it):
                pe.wait_ge(sem("att_p"), it + 1)
                if it >= 1:
                    pe.wait_ge(sem("att_turned"), it)
                for n, _ in enumerate(att_blocks(it)):
                    mm = nc.tensor.transpose(banks[n // 4][:, (n % 4) * P:(n % 4 + 1) * P],
                                             SC[:, it % 2, n * P:(n + 1) * P], ident)
                mm.then_inc(sem("att_t"), 1)

            def weigh(it):
                hh, c = it // TC, it % TC
                pe.wait_ge(sem("att_turned"), it + 1)
                if it == 2 * TC:
                    pe.wait_ge(sem("tmp_ready"), splits["y_attn"][0] + 1)
                b = 64 * (hh % 2)
                bl = att_blocks(it)
                for n, (g, kc) in enumerate(bl):
                    head = 4 * g + hh
                    mm = nc.tensor.matmul(banks[7][b:b + 64, c * P:(c + 1) * P], VT[:, kc, 64 * head:64 * head + 64],
                                          PT[:, n * P:(n + 1) * P], start=(n == 0), stop=(n == len(bl) - 1))
                mm.then_inc(sem("att_y"), 1)

            for it in range(4 * TC + 1):
                if it < 4 * TC:
                    scores(it)
                if it >= 1:
                    turn(it - 1)
                    weigh(it - 1)

            stage("lora", "n_mix")
            pe.wait_ge(sem("lora_ready"), 3)

            def group(name, p, last):
                last.then_inc(sem("rw_made"), 1)

            def start_group(name, p):
                n = p * len(STEPS) + INDEX[name] - 4
                if n >= 0:
                    emptied(pe, STEPS[n % len(STEPS)][0], n // len(STEPS))
                return rbank(name, p)

            def expanded(name, p, h, lhs, rhs, w=P):
                b = start_group(name, p)
                for i in range(4):
                    c = 4 * h + i
                    mm = nc.tensor.matmul(b[:, w * i:w * (i + 1)], lhs[:, c, :],
                                          rhs(c), start=True, stop=True)
                mm.then_inc(sem("rw_made"), 1)

            def turned(name, p, h, src):
                b = start_group(name, p)
                for i in range(4):
                    mm = nc.tensor.transpose(b[:, P * i:P * (i + 1)], src[:, 4 * h + i, :], ident)
                mm.then_inc(sem("rw_made"), 1)

            stage("rkv0", "n_mix")
            for p in range(PAIRS):
                ahead = list(range(*stages[f"rkv{p + 1}"])) if p + 1 < PAIRS else []
                pe.wait_ge(sem(f"lw_landed"), 16 * (p + 1))
                b = start_group("zw", p)
                nc.tensor.matmul(b[:], LW[0:64, 0, :], LORA[0:64, :], start=True, stop=True).then_inc(sem("rw_made"), 1)
                b = start_group("za", p)
                nc.tensor.matmul(b[:], LW[64:128, 0, :], LORA[64:128, :], start=True,
                                 stop=True).then_inc(sem("rw_made"), 1)
                b = start_group("zg", p)
                nc.tensor.matmul(b[:], LW[:, 1, :], GD[:, 0, :], start=True, stop=False)
                nc.tensor.matmul(b[:], LW[:, 2, :], GD[:, 1, :], start=False, stop=True).then_inc(sem("rw_made"), 1)
                b = start_group("ss", p)
                pe.wait_ge(sem("rw_kk_sq"), p + 1)
                nc.tensor.matmul(b[:], heads, RK, start=True, stop=True).then_inc(sem("rw_made"), 1)
                b = start_group("bonus", p)
                pe.wait_ge(sem("rw_rk"), p + 1)
                nc.tensor.matmul(b[:], heads, RK, start=True, stop=True).then_inc(sem("rw_made"), 1)
                pe.wait_ge(sem("rw_ar"), p + 1)
                for h in range(2):
                    expanded(f"bM{h}", p, h, BX, lambda c: AR[:, c, :, :])
                    expanded(f"kM{h}", p, h, KX, lambda c: AR[:, c, :, :])
                for h in range(2):
                    pe.wait_ge(sem("rw_tt0"), 2 * p + h + 1)
                    turned(f"tT{h}", p, h, TTX)
                    if h == 0:
                        pe.wait_ge(sem("rw_ax"), p + 1)
                    turned(f"tA{h}", p, h, AX)
                for h in range(2):
                    turned(f"tB{h}", p, h, BX)
                    turned(f"tV{h}", p, h, VX)
                for l in range(1, 6):
                    for h in range(2):
                        if l == 1:
                            emptied(pe, f"tT{h}", p)
                            emptied(pe, f"tA{h}", p)
                        else:
                            emptied(pe, f"D{l - 1}{h}", p)
                        expanded(f"P{l}{h}", p, h, LAB, lambda c: TX[:, c, :])
                    if ahead:
                        tile(ahead.pop(0), splits["n_mix"][0])
                    for h in range(2):
                        emptied(pe, f"P{l}{h}", p)
                        if l > 1:
                            emptied(pe, f"X{l - 1}{h}", p)
                        expanded(f"D{l}{h}", p, h, TTX, lambda c: PX[:, c, :])
                    for h in range(2):
                        emptied(pe, f"D{l}{h}", p)
                        turned(f"X{l}{h}", p, h, TX)
                    if l == 1:
                        for h in range(2):
                            turned(f"tK{h}", p, h, KX)
                        for h in range(2):
                            emptied(pe, f"tV{h}", p)
                            expanded(f"Z{h}", p, h, LAK, lambda c: VC[:, c, :], CH)
                for h in range(2):
                    emptied(pe, f"X5{h}", p)
                    emptied(pe, f"Z{h}", p)
                    expanded(f"TAX{h}", p, h, TTX, lambda c: AZ[:, c, :, :])
                for h in range(2):
                    emptied(pe, f"TAX{h}", p)
                    emptied(pe, f"tB{h}", p)
                    expanded(f"RM{h}", p, h, TAX, lambda c: RM[:, c, :, :])
                for h in range(2):
                    emptied(pe, f"tK{h}", p)
                    b = start_group(f"N{h}", p)
                    for i in range(4):
                        c = 4 * h + i
                        nc.tensor.matmul(b[:, CH * i:CH * (i + 1)], BX[:, c, :], X0C[:, c, :], start=True, stop=False)
                        mm = nc.tensor.matmul(b[:, CH * i:CH * (i + 1)], KX[:, c, :], VC[:, c, :], start=False,
                                              stop=True)
                    mm.then_inc(sem("rw_made"), 1)
                b = start_group("scan", p)
                emptied(pe, "N1", p)
                for c in range(1, NC - 1):
                    pe.wait_ge(sem("rw_state"), p * (NC - 2) + c)
                    mm = nc.tensor.matmul(b[:, CH * c:CH * (c + 1)], MCX[:, c, :], SC_[:, c, :], start=True, stop=True)
                    mm.then_inc(sem("rw_made" if c == NC - 2 else "rw_stepped"), 1)
                b = start_group("Y", p)
                pe.wait_ge(sem("rw_sx"), p + 1)
                for c in range(NC):
                    o = b[:, CH * c:CH * (c + 1)]
                    nc.tensor.matmul(o, X0X[:, c, :], RM[:, c, 0, :], start=True, stop=False)
                    mm = nc.tensor.matmul(o, VX[:, c, :], MRK[:, c, :], start=False, stop=(c == 0))
                    if c:
                        mm = nc.tensor.matmul(o, SX[:, c, :], AR[:, c, 1, :], start=False, stop=True)
                mm.then_inc(sem("rw_made"), 1)
                while ahead:
                    tile(ahead.pop(0), splits["n_mix"][0])
                b = start_group("mean", p)
                emptied(pe, "Y", p)
                nc.tensor.matmul(b[:], heads, K, start=True, stop=True).then_inc(sem("rw_made"), 1)
                b = start_group("var", p)
                pe.wait_ge(sem("rw_ysq"), p + 1)
                nc.tensor.matmul(b[:], heads, YSQ, start=True, stop=True).then_inc(sem("rw_made"), 1)

            stage("attn_out", "y_attn")
            stage("gate_a", "n_mix")
            pair_stage("rwkv_out", "n_mix", "y_rwkv")
            stage("mix_out", "merged")
            for j in range(KT):
                sum_squares("mem", j, M)
            stage("mem_k", "n_mem", M)
            stage("mem_v", "n_mem")
            for j in range(KT):
                sum_squares("x", j)
            stage("x_q", "n_x")
            all_evacuated(pe, "x_q")
            for hd in range(XH):
                if hd:
                    pe.wait_ge(sem("x_scored"), hd)
                for c in range(TC):
                    for k in range(2):
                        mm = nc.tensor.matmul(banks[4 + c // 2][:, M * (c % 2):M * (c % 2 + 1)],
                                              XQ[:, 2 * hd + k, c * P:(c + 1) * P], KM[:, 2 * hd + k, :],
                                              start=(k == 0), stop=(k == 1))
                mm.then_inc(sem("x_raw"), 1)
                pe.wait_ge(sem("x_p"), hd + 1)
                if hd:
                    pe.wait_ge(sem("x_turned"), hd)
                for m in range(2):
                    for c in range(TC):
                        mm = nc.tensor.transpose(banks[m][:, c * P:(c + 1) * P], XP[:, c, m * P:(m + 1) * P], ident)
                mm.then_inc(sem("x_t"), 1)
                pe.wait_ge(sem("x_turned"), hd + 1)
                if hd:
                    pe.wait_ge(sem("tmp_ready"), splits["x_o"][0] + 2 * hd)
                for d in range(2):
                    for m in range(2):
                        mm = nc.tensor.matmul(banks[6 + d][:], VM[:, m, 256 * hd + P * d:256 * hd + P * (d + 1)],
                                              XPT[:, m, :], start=(m == 0), stop=(m == 1))
                mm.then_inc(sem("x_y"), 1)
            stage("x_out", "x_o", norm="ffn")

            def modulation(n):
                for i in (2 * n, 2 * n + 1):
                    if i == 0:
                        pe.wait_ge(sem("c_ready"), 1)
                    pe.wait_ge(sem(f"ada_landed{i % 4}"), 16 * (i // 4 + 1))
                    for k in range(KT):
                        mm = nc.tensor.matmul(banks[5][:, i:i + 1], ADA_W[:, i % 4, k * P:(k + 1) * P],
                                              c_act[:, k:k + 1], start=(k == 0), stop=(k == KT - 1))
                    mm.then_inc(sem("ada_used"), 1)

            t_ada = ADA_TILES[0]
            for c, _ in enumerate(chunks_of(FF1)):
                for name, split in ((f"up{c}", "n_ffn"), (f"down{c}", f"hidden{c}")):
                    for t in range(*stages[name]):
                        tile(t, splits[split][0])
                        if t - t_ada < ADA:
                            modulation(t - t_ada)
                        if name == "down3" and t > stages[name][0]:
                            sum_squares("final", t - stages[name][0] - 1)
            sum_squares("final", KT - 1)

            for l in range(LAYERS):
                for j in range(KT):
                    sum_squares(f"n1_{l}", j)
                if l == 0:
                    pass
                t0 = stages[f"fourier_in{l}"][0]
                pe.wait_ge(sem("fourier_tables"), 48 * (l + 1))

                def fourier_group(j):
                    g = KT * l + j
                    evacuated(pe, t0 + j)
                    if g >= 1:
                        pe.wait_ge(sem("f_half"), 2 * g)
                    for c in range(TC):
                        mm = nc.tensor.matmul(banks[4 + c // 2][:, 256 * (c % 2):256 * (c % 2 + 1)],
                                              UF[:, j % 2, c * P:(c + 1) * P], CS_FEAT, start=True, stop=True)
                    mm.then_inc(sem("f_feat"), 1)

                def fourier_tokens(j):
                    g = KT * l + j
                    pe.wait_ge(sem("f_half"), 2 * g + 2)
                    if j >= 2:
                        pe.wait_ge(sem("tmp_ready"), splits[f"fourier{l}"][0] + j - 1)
                    elif l:
                        pass
                    for c in range(TC):
                        nc.tensor.matmul(banks[6 + j % 2][:], PF[:, j % 2, c, 0:P], CS_SEQ[:, c, :], start=(c == 0),
                                         stop=False)
                        mm = nc.tensor.matmul(banks[6 + j % 2][:], PF[:, j % 2, c, P:2 * P], SN_SEQ[:, c, :],
                                              start=False, stop=(c == TC - 1))
                    mm.then_inc(sem("f_made"), 1)

                for j in range(KT):
                    tile(t0 + j, splits[f"n1_{l}"][0])
                    if j >= 1:
                        fourier_group(j - 1)
                    if j >= 2:
                        fourier_tokens(j - 2)
                fourier_group(KT - 1)
                fourier_tokens(KT - 2)
                fourier_tokens(KT - 1)
                pair_stage(f"fourier_out{l}", f"n1_{l}", f"fourier{l}")
                def head_tiles(hd, what):
                    for t in range(*stages[f"ret_{what}{l}_{hd}"]):
                        tile(t, splits[f"n1_{l}"][0])

                head_tiles(0, "q")
                head_tiles(0, "k")
                for hd in range(XH):
                    n = XH * l + hd
                    head_tiles(hd, "v")
                    head_tiles(hd, "g")
                    pe.wait_ge(sem("rotated"), 2 * n + 2)
                    for c in range(TC):
                        if TC * n + c >= 2:
                            pe.wait_ge(sem("ret_masked"), TC * n + c - 1)
                        for k in range(2):
                            mm = nc.tensor.matmul(banks[4 + c % 2][:], RKY[:, k, c * P:(c + 1) * P],
                                                  RQ[:, k, :], start=(k == 0), stop=(k == 1))
                        mm.then_inc(sem("ret_raw"), 1)
                    if hd + 1 < XH:
                        head_tiles(hd + 1, "q")
                    all_evacuated(pe, f"ret_v{l}_{hd}")
                    pe.wait_ge(sem("ret_masked"), TC * (n + 1))
                    if n:
                        pe.wait_ge(sem("ret_std"), n)
                    for d in range(2):
                        for c in range(TC):
                            mm = nc.tensor.matmul(banks[6 + d][:], RV[:, c, P * d:P * (d + 1)], RP[:, c, :],
                                                  start=(c == 0), stop=(c == TC - 1))
                        mm.then_inc(sem("ret_y"), 1)
                    if hd + 1 < XH:
                        tile(stages[f"ret_k{l}_{hd + 1}"][0], splits[f"n1_{l}"][0])
                    pe.wait_ge(sem("ret_copied"), 2 * n + 2)
                    for d in range(2):
                        mm = nc.tensor.matmul(banks[6][:], ones, RY[:, d, :], start=(d == 0), stop=(d == 1))
                    mm.then_inc(sem("ret_mean"), 1)
                    if hd + 1 < XH:
                        tile(stages[f"ret_k{l}_{hd + 1}"][0] + 1, splits[f"n1_{l}"][0])
                    pe.wait_ge(sem("ret_sq"), 2 * n + 2)
                    for d in range(2):
                        mm = nc.tensor.matmul(banks[7][:], ones, ROT[:, 2 + d, :], start=(d == 0), stop=(d == 1))
                    mm.then_inc(sem("ret_var"), 1)
                pair_stage(f"ret_out{l}", f"n1_{l}", f"ret{l}")
                stage(f"out{l}", f"m{l}", norm=f"n2_{l}")
                for c, _ in enumerate(chunks_of(FF2)):
                    stage(f"ff_in{l}_{c}", f"n2_{l}")
                    last = c == len(chunks_of(FF2)) - 1
                    stage(f"ff_out{l}_{c}", f"ff{l}_{c}", norm="out" if last and l == LAYERS - 1 else None)

        @block.scalar
        def _(act):
            ahead = [0]
            counts = {}

            def done(ins, signal, wait=False):
                counts[signal] = counts.get(signal, 0) + 1
                ins.then_inc(sem(signal), 1)
                if wait:
                    act.wait_ge(sem(signal), counts[signal])

            def follow(t):
                last = min(max(u for u, _, _ in tiles[t]["blocks"]) + 2, n_units - 1)
                if t == len(tiles) - 1:
                    last = n_units - 1
                while ahead[0] <= last:
                    u, k = ahead[0], ahead[0] % RING
                    act.wait_ge(sem(f"w_landed{k}"), 16 * (u // RING + 1))
                    if u >= RING:
                        act.wait_ge(sem("tile_done"), last_tile[u - RING] + 1)
                    nc.scalar.copy(w_hi[:, k, :], w_raw[:, k, :]).then_inc(sem("w_high"), 1)
                    ahead[0] += 1

            def take_tile(t, dst, n=S, func=ACT.Copy, scale=1.0, b0=0):
                follow(t)
                tile_done(act, t)
                nc.scalar.activation(dst, banks[t % BANKS][:, 0:n], func, scale=scale).then_inc(
                    sem(f"bank_free{t % BANKS}"), 1)

            def follow_stage(name, split=None):
                t0, t1 = stages[name]
                q = splits[split][0] if split else None
                for t in range(t0, t1):
                    follow(t)
                    if split:
                        high(q + t - t0)

            def high(q):
                buf, j, free_after = conv[q]
                act.wait_ge(sem("tmp_ready"), q + 1)
                if free_after:
                    tile_done(act, free_after - 1)
                n = M if splits["n_mem"][0] <= q < splits["n_mem"][1] else S
                nc.scalar.copy(acts[buf][:, 0, j, 0:n], tmp[:, q % 2, 0:n]).then_inc(sem("high_done"), 1)

            def highs(split):
                for q in range(*splits[split]):
                    high(q)

            def square(name, j, src, n=S):
                s = squares_before(name) + j
                if s >= 2:
                    act.wait_ge(sem("sq_used"), s - 1)
                nc.scalar.activation(squares[:, s % 2, 0:n], src, ACT.Square).then_inc(sem("sq_ready"), 1)

            def deviation(name, n=S):
                act.wait_ge(sem("sum_read"), NORMS.index(name) + 1)
                nc.scalar.activation(rstd[:, 0:n], rstd[:, 0:n], ACT.Sqrt).then_inc(sem("rms_ready"), 1)

            act.dma_start(table[:], ap["table"]).then_inc(sem("ld_table"), 16)
            act.dma_start(H, ap["x"]).then_inc(sem("ld_x"), 16)
            act.dma_start(params[:], ap["params"]).then_inc(sem("ld_params"), 16)
            act.dma_start(DIST, ap["dist"]).then_inc(sem("ld_dist"), 16)
            act.wait_ge(sem("ld_x"), 16)
            for j in range(KT):
                square("mix", j, H[:, j, :])
            follow(0)
            deviation("mix")
            highs("n_mix")
            for t in range(*stages["qk"]):
                j = t - stages["qk"][0]
                take_tile(t, QK[:, j, :], scale=0.125 if j < 6 else 1.0)
            for t in range(*stages["v"]):
                T = tiles[t]
                take_tile(t, VT[:, T["token"], T["col"]:T["col"] + T["width"]], T["width"])
            q_attn = splits["y_attn"][0]

            def turned_out(it):
                act.wait_ge(sem("att_t"), it + 1)
                if it:
                    act.wait_ge(sem("att_y"), it)
                c = it % TC
                nb = (c + 1) * 2 + min(c + 1, 2)
                for i in range((nb + 3) // 4):
                    w = min(4, nb - 4 * i) * P
                    ins = nc.scalar.copy(PT[:, 512 * i:512 * i + w], banks[i][:, 0:w])
                done(ins, "att_turned")

            for it in range(4 * TC):
                c = it % TC
                act.wait_ge(sem("att_max"), it + 1)
                nb = (c + 1) * 2 + min(c + 1, 2)
                done(nc.scalar.activation(SC[:, it % 2, 0:nb * P], SC[:, it % 2, 0:nb * P], ACT.Exp,
                                          bias=att_stat[:, it % 2, 0:1], scale=1.0,
                                          accum_out=att_stat[:, it % 2, 1:2]), "att_exp")
                if it >= 1:
                    turned_out(it - 1)
                if it == 2 * TC + 2:
                    high(q_attn)
            turned_out(4 * TC - 1)
            high(q_attn + 1)

            def to_raw(t, i):
                if i >= 2:
                    act.wait_ge(sem("shift_done"), i - 1)
                take_tile(t, RAW[:, i % 2, 8:8 + S])

            act.wait_ge(sem("rw_zeroed"), 1)
            for p in range(1):
                act.dma_start(LW, ap["lora_w"][p]).then_inc(sem("lw_landed"), 16)
            for i in range(3):
                to_raw(stages["lora"][0] + i, i)
                act.wait_ge(sem("shift_done"), i + 1)
                if i == 0:
                    done(nc.scalar.activation(LORA[0:64, :], LORA[0:64, :], ACT.Tanh), "lora_ready")
                else:
                    done(nc.scalar.activation(GD[:, i - 1, :], GD[:, i - 1, :], ACT.Sigmoid), "lora_ready")
            for i in range(3):
                to_raw(stages["rkv0"][0] + i, 3 + i)

            for p in range(PAIRS):
                def ready(name):
                    act.wait_ge(sem(name), p + 1)

                def out_of(name, dst, src=None, last=True, **kw):
                    ins = nc.scalar.activation(dst, rbank(name, p)[:] if src is None else src, **kw)
                    if last:
                        ins.then_inc(sem("rw_emptied_a"), 1)

                made(act, "zw", p)
                out_of("zw", SW, func=ACT.Sigmoid, bias=prm("w0", p))
                made(act, "za", p)
                out_of("za", A_, func=ACT.Sigmoid, bias=prm("a0", p))
                made(act, "zg", p)
                out_of("zg", G, func=ACT.Copy)
                ready("rw_kk")
                done(nc.scalar.activation(RK, KK, ACT.Square), "rw_kk_sq")
                emptied(act, "ss", p)
                done(nc.scalar.activation(DIFF, DIFF, ACT.Sqrt), "rw_norm")
                ready("rw_cs")
                nc.scalar.activation(W, CS, ACT.Exp, scale=LOG_DECAY)
                nc.scalar.activation(WI, CS, ACT.Exp, scale=-LOG_DECAY)
                done(nc.scalar.activation(WX, WX, ACT.Exp, scale=LOG_DECAY), "rw_w")
                ready("rw_ar")
                for h in range(2):
                    r = slice(64 * h, 64 * h + 64)
                    nc.scalar.copy(AX[r, :, 64 * h:64 * h + 64], AR[r, :, 0, :])
                    ins = nc.scalar.copy(VX[r, :, 64 * h:64 * h + 64], V[r, :].rearrange("p (c t) -> p c t", t=CH))
                done(ins, "rw_ax")

                def halves(name, h, wide, compact):
                    made(act, name, p)
                    src = rbank(name, p)[:].rearrange("p (c s) -> p c s", s=P)
                    cs = slice(4 * h, 4 * h + 4)
                    if wide is not None:
                        out_of(name, wide[:, cs, :], src, last=compact is None, func=ACT.Copy)
                    if compact is not None:
                        for i in range(2):
                            r = slice(64 * i, 64 * i + 64)
                            out_of(name, compact[r, cs, :], src[r, :, 64 * i:64 * i + 64], last=i == 1, func=ACT.Copy)

                for h in range(2):
                    halves(f"tT{h}", h, TX, None)
                    halves(f"tA{h}", h, None, AZ[:, :, 0, :])
                for h in range(2):
                    halves(f"tB{h}", h, BX, RM[:, :, 1, :])
                    halves(f"tV{h}", h, VX, VC)
                nxt = list(range(*stages[f"rkv{p + 1}"])) if p + 1 < PAIRS else []
                for l in range(1, 6):
                    if nxt:
                        follow(nxt.pop(0))
                    for h in range(2):
                        halves(f"X{l}{h}", h, TTX, None)
                    if l == 1:
                        for h in range(2):
                            halves(f"tK{h}", h, KX, None)
                        for h in range(2):
                            made(act, f"Z{h}", p)
                            out_of(f"Z{h}", AZ[:, 4 * h:4 * h + 4, 1, :],
                                   rbank(f"Z{h}", p)[:, 0:256].rearrange("p (c s) -> p c s", s=CH), func=ACT.Copy)
                made(act, "Y", p)
                out_of("Y", K, func=ACT.Copy)
                if p + 1 < PAIRS:
                    act.dma_start(LW, ap["lora_w"][p + 1]).then_inc(sem("lw_landed"), 16)
                emptied(act, "mean", p)
                done(nc.scalar.activation(YSQ, YC, ACT.Square), "rw_ysq")
                emptied(act, "var", p)
                done(nc.scalar.activation(WI, WI, ACT.Sqrt), "rw_std")
                high(splits["y_rwkv"][0] + p)
                if p + 1 < PAIRS:
                    for i in range(3):
                        to_raw(stages[f"rkv{p + 1}"][0] + i, 3 + 3 * (p + 1) + i)

            act.wait_ge(sem("low_done"), splits["y_rwkv"][1])
            act.dma_start(H, ap["x"]).then_inc(sem("ld_x"), 16)
            act.dma_start(MEM, ap["mem"]).then_inc(sem("ld_mem"), 16)
            follow_stage("attn_out")

            def gates(name, t_gates, each=1):
                for t in t_gates:
                    i = counts.get("gate_ready", 0)
                    if i >= 2:
                        act.wait_ge(sem("gate_used"), i - 1)
                    follow(t)
                    tile_done(act, t)
                    nc.scalar.activation(gate_buf[:, i % 2, :], banks[t % BANKS][:], ACT.Sigmoid).then_inc(
                        sem(f"bank_free{t % BANKS}"), 1)
                    counts["gate_ready"] = i + 1
                    if each == 2:
                        follow(t + 1)

            gates("gate_a", range(*stages["gate_a"]))
            gates("rwkv_out", range(stages["rwkv_out"][0], stages["rwkv_out"][1], 2), 2)
            highs("merged")
            follow_stage("mix_out")
            act.wait_ge(sem("ld_mem"), 16)
            for j in range(KT):
                square("mem", j, MEM[:, j, :], M)
            deviation("mem", M)
            highs("n_mem")
            for t in range(*stages["mem_k"]):
                take_tile(t, KM[:, t - stages["mem_k"][0], :], M)
            for t in range(*stages["mem_v"]):
                T = tiles[t]
                take_tile(t, VM[:, T["token"], T["col"]:T["col"] + T["width"]], T["width"])
            for j in range(KT):
                square("x", j, H[:, j, :])
            deviation("x")
            highs("n_x")
            for t in range(*stages["x_q"]):
                take_tile(t, XQ[:, t - stages["x_q"][0], :], scale=1.0 / 16)
            for hd in range(XH):
                act.wait_ge(sem("x_max"), hd + 1)
                for c in range(TC):
                    ins = nc.scalar.activation(XP[:, c, :], banks[4 + c // 2][:, M * (c % 2):M * (c % 2 + 1)], ACT.Exp,
                                               bias=x_stat[:, c, 0:1], scale=1.0, accum_out=x_stat[:, c, 1:2])
                done(ins, "x_scored")
                act.wait_ge(sem("x_t"), hd + 1)
                if hd:
                    act.wait_ge(sem("x_y"), hd)
                for m in range(2):
                    ins = nc.scalar.copy(XPT[:, m, :], banks[m][:])
                done(ins, "x_turned")
                for d in range(2):
                    high(splits["x_o"][0] + 2 * hd + d)
            t0 = stages["x_out"][0]
            act.wait_ge(sem("ld_params"), 16)
            done(nc.scalar.activation(c_act, prm("c", 0, 8), ACT.Silu), "c_ready")
            for t in range(*stages["x_out"]):
                follow(t)
                evacuated(act, t)
                square("ffn", t - t0, H[:, t - t0, :])
            deviation("ffn")
            highs("n_ffn")
            for c, _ in enumerate(chunks_of(FF1)):
                q = splits[f"hidden{c}"][0]
                t0, t1 = stages[f"up{c}"]
                for t in range(t0, t1):
                    i = 8 * c + t - t0
                    follow(t)
                    tile_done(act, t)
                    if t - t0 >= 2:
                        act.wait_ge(sem("tmp_ready"), q + t - t0 - 1)
                    nc.scalar.activation(RELU[:, i % 2, :], banks[t % BANKS][:], ACT.Relu).then_inc(
                        sem(f"bank_free{t % BANKS}"), 1)
                    if t > t0:
                        high(q + t - t0 - 1)
                high(q + t1 - t0 - 1)
                t0, t1 = stages[f"down{c}"]
                for t in range(t0, t1):
                    follow(t)
                    if c == 3:
                        evacuated(act, t)
                        square("final", t - t0, H[:, t - t0, :])
            deviation("final")

            for l in range(LAYERS):
                for j in range(KT):
                    if l == 0:
                        act.wait_ge(sem("final_done"), j + 1)
                    square(f"n1_{l}", j, H[:, j, :])
                act.dma_start(CS_SEQ, ap["dft_cos"]).then_inc(sem("fourier_tables"), 16)
                act.dma_start(SN_SEQ, ap["dft_sin"]).then_inc(sem("fourier_tables"), 16)
                act.dma_start(CS_FEAT, ap["dft_feature"]).then_inc(sem("fourier_tables"), 16)
                deviation(f"n1_{l}")
                highs(f"n1_{l}")
                t0 = stages[f"fourier_in{l}"][0]
                for j in range(KT + 2):
                    if j < KT:
                        if KT * l + j >= 2:
                            act.wait_ge(sem("f_feat"), KT * l + j - 1)
                        take_tile(t0 + j, UF[:, j % 2, :])
                    if 1 <= j <= KT:
                        g = KT * l + j - 1
                        act.wait_ge(sem("f_feat"), g + 1)
                        if g >= 2:
                            act.wait_ge(sem("f_made"), g - 1)
                        for i in range(2):
                            done(nc.scalar.copy(PF[:, (j - 1) % 2, 2 * i:2 * i + 2, :],
                                                banks[4 + i][:].rearrange("p (c f) -> p c f", f=256)), "f_half")
                    if j >= 2:
                        high(splits[f"fourier{l}"][0] + j - 2)
                gates("", range(stages[f"fourier_out{l}"][0], stages[f"fourier_out{l}"][1], 2), 2)
                for hd in range(XH):
                    n = XH * l + hd
                    for what in "qk":
                        for t in range(*stages[f"ret_{what}{l}_{hd}"]):
                            follow(t)
                    if hd == 0:
                        act.wait_ge(sem("gate_used"), counts["gate_ready"])
                        act.dma_start(COS, ap["rotary"][:, 0, :]).then_inc(sem("ret_tables"), 16)
                        act.dma_start(SIN, ap["rotary"][:, 1, :]).then_inc(sem("ret_tables"), 16)
                    else:
                        act.wait_ge(sem("ret_masked"), TC * n)
                    act.dma_start(STRIP, ap["strips"][hd]).then_inc(sem("strip_landed"), 16)
                    t0 = stages[f"ret_v{l}_{hd}"][0]
                    if n:
                        act.wait_ge(sem("ret_y"), 2 * n)
                    for t in range(t0, t0 + TC):
                        take_tile(t, RV[:, t - t0, :], 256)
                    for t in range(*stages[f"ret_g{l}_{hd}"]):
                        i = t - stages[f"ret_g{l}_{hd}"][0]
                        if n:
                            act.wait_ge(sem("tmp_ready"), splits[f"ret{l}"][0] + 2 * hd)
                        take_tile(t, RG[:, i, :], func=ACT.Silu)
                    if hd + 1 < XH:
                        for t in range(*stages[f"ret_q{l}_{hd + 1}"]):
                            follow(t)
                    for d in range(2):
                        act.wait_ge(sem("ret_y"), 2 * n + d + 1)
                        done(nc.scalar.copy(RY[:, d, :], banks[6 + d][:]), "ret_copied")
                    if hd + 1 < XH:
                        for t in range(*stages[f"ret_k{l}_{hd + 1}"]):
                            follow(t)
                    for d in range(2):
                        act.wait_ge(sem("ret_centred"), 2 * n + d + 1)
                        done(nc.scalar.activation(ROT[:, 2 + d, :], RY[:, d, :], ACT.Square), "ret_sq")
                    act.wait_ge(sem("ret_var_read"), n + 1)
                    done(nc.scalar.activation(ROT[:, 0, :], ROT[:, 0, :], ACT.Sqrt), "ret_std")
                    for d in range(2):
                        high(splits[f"ret{l}"][0] + 2 * hd + d)
                gates("", range(stages[f"ret_out{l}"][0], stages[f"ret_out{l}"][1], 2), 2)
                highs(f"m{l}")
                t0 = stages[f"out{l}"][0]
                for t in range(*stages[f"out{l}"]):
                    follow(t)
                    evacuated(act, t)
                    square(f"n2_{l}", t - t0, H[:, t - t0, :])
                deviation(f"n2_{l}")
                highs(f"n2_{l}")
                for c, (a, n) in enumerate(chunks_of(FF2)):
                    t0 = stages[f"ff_in{l}_{c}"][0]
                    q = splits[f"ff{l}_{c}"][0]
                    for j in range(n):
                        i = FF2 * l + a + j
                        for half in range(2):
                            if 2 * i + half >= 2:
                                act.wait_ge(sem("conv_done"), 2 * i + half - 1)
                            take_tile(t0 + 2 * j + half, FRAW[:, half, 8:8 + S])
                        act.wait_ge(sem("conv_done"), 2 * i + 1)
                        done(nc.scalar.activation(CONV[:, i % 2, 0, :], CONV[:, i % 2, 0, :], ACT.Gelu), "gelu")
                        if j:
                            high(q + j - 1)
                    high(q + n - 1)
                    t0 = stages[f"ff_out{l}_{c}"][0]
                    for t in range(t0, t0 + 8):
                        follow(t)
                        if l == LAYERS - 1 and c == len(chunks_of(FF2)) - 1:
                            evacuated(act, t)
                            square("out", t - t0, H[:, t - t0, :])
                if l == LAYERS - 1:
                    deviation("out")
                else:
                    all_evacuated(act, f"ff_out{l}_{len(chunks_of(FF2)) - 1}")

        @block.vector
        def _(dve):
            counts = {}
            V_ = nc.vector

            def do(ins, signal="vector_step", value=None):
                if value is None:
                    value = counts[signal] = counts.get(signal, 0) + 1
                ins.then_inc(sem(signal), 1)
                dve.wait_ge(sem(signal), value)

            def take_tile(t, make_op):
                tile_done(dve, t)
                do(make_op(banks[t % BANKS]), f"bank_free{t % BANKS}", t // BANKS + 1)

            def low(q):
                buf, j, _ = conv[q]
                n = M if splits["n_mem"][0] <= q < splits["n_mem"][1] else S
                dve.wait_ge(sem("high_done"), q + 1)
                do(V_.tensor_tensor(acts[buf][:, 1, j, 0:n], tmp[:, q % 2, 0:n],
                                    acts[buf][:, 0, j, 0:n].bitcast(F32), ALU.subtract), "low_done")

            def split_all(split, make_op):
                q0, q1 = splits[split]
                for q in range(q0, q1):
                    make_op(q - q0, tmp[:, q % 2, :])
                    if q > q0:
                        low(q - 1)
                low(q1 - 1)

            def inverse_deviation(name, n=S):
                k = NORMS.index(name)
                dve.wait_ge(sem("sq_used"), squares_before(name) + KT)
                do(V_.tensor_scalar(rstd[:, 0:n], banks[4][:, 0:n], 1.0 / D, EPS, ALU.mult, ALU.add), "sum_read")
                dve.wait_ge(sem("rms_ready"), k + 1)
                do(V_.reciprocal(rstd[:, 0:n], rstd[:, 0:n]))

            def scaled_by(dst, src, g, signal, n=S):
                do(V_.scalar_tensor_tensor(dst, src, g, rstd[:, 0:n], ALU.mult, ALU.mult), signal)

            def add_to_h(t, j, scale=None):
                if scale is None:
                    take_tile(t, lambda b: V_.tensor_tensor(H[:, j, :], H[:, j, :], b[:], ALU.add))
                else:
                    take_tile(t, lambda b: V_.scalar_tensor_tensor(H[:, j, :], b[:], scale, H[:, j, :], ALU.mult,
                                                                   ALU.add))

            dve.wait_ge(sem("ld_x"), 16)
            dve.wait_ge(sem("ld_params"), 16)
            inverse_deviation("mix")
            split_all("n_mix", lambda j, d: scaled_by(d, H[:, j, :], prm("g_mix", j), "tmp_ready"))

            dve.wait_ge(sem("ld_dist"), 16)
            q_attn = splits["y_attn"][0]

            def weights(it):
                dve.wait_ge(sem("att_exp"), it + 1)
                w = ((it % TC + 1) * 2 + min(it % TC + 1, 2)) * P
                st = att_stat[:, it % 2, :]
                do(V_.reciprocal(st[:, 2:3], st[:, 1:2]))
                do(V_.tensor_scalar(SC[:, it % 2, 0:w], SC[:, it % 2, 0:w], st[:, 2:3], None, ALU.mult), "att_p")

            for it in range(4 * TC):
                hh, c = it // TC, it % TC
                dve.wait_ge(sem("att_raw"), it + 1)
                if it >= 2:
                    dve.wait_ge(sem("att_t"), it - 1)
                at = 0
                for g in range(3):
                    w = (min(c + 1, 2) if g == 0 else c + 1) * P
                    d_end = (256, 768, 1280)[g]
                    do(V_.scalar_tensor_tensor(SC[:, it % 2, at:at + w], DIST[:, d_end - w:d_end],
                                               -float(2.0 ** (-8.0 * (4 * g + hh + 1) / AH)), banks[4 + g][:, 0:w],
                                               ALU.mult, ALU.add), "att_scored" if g == 2 else "vector_step")
                    at += w
                do(V_.tensor_reduce(att_stat[:, it % 2, 0:1], SC[:, it % 2, 0:at], AX_X, ALU.max, negate=True),
                   "att_max")
                if it >= 1:
                    weights(it - 1)
                if it == 2 * TC + 1:
                    dve.wait_ge(sem("att_y"), 2 * TC)
                    do(V_.tensor_copy(tmp[:, q_attn % 2, :], banks[7][:]), "tmp_ready")
            weights(4 * TC - 1)
            low(q_attn)
            dve.wait_ge(sem("att_y"), 4 * TC)
            do(V_.tensor_copy(tmp[:, (q_attn + 1) % 2, :], banks[7][:]), "tmp_ready")
            low(q_attn + 1)

            for a in (BX, KX, VX, AX, RAW):
                do(V_.memset(a, 0.0))
            do(V_.memset(LORA[:, 0:8], 0.0), "rw_zeroed")

            def shift(t, i, mu, dst):
                evacuated(dve, t)
                raw = RAW[:, i % 2, :]
                do(V_.tensor_tensor(DIFF, raw[:, 7:7 + S], raw[:, 8:8 + S], ALU.subtract))
                do(V_.scalar_tensor_tensor(dst, DIFF, prm("mu", mu), raw[:, 8:8 + S], ALU.mult, ALU.add), "shift_done")

            for i, dst in enumerate((LORA, GD[:, 0, :], GD[:, 1, :])):
                shift(stages["lora"][0] + i, i, 24 + i, dst)

            def by_chunk(a):
                return a.rearrange("p (c t) -> p c t", t=CH)

            def four(a):
                return a[:].rearrange("p (c s) -> p c s", s=P)

            def twice(a):
                return a.unsqueeze(2).to_broadcast([P, 4, 2, CH])

            def both(a):
                return a.rearrange("p c (h s) -> p c h s", h=2)

            def mask2(m):
                return m.rearrange("p (h s) -> p h s", h=2).unsqueeze(1).to_broadcast([P, 4, 2, CH])

            def mask1(m):
                return m.unsqueeze(1).to_broadcast([P, 4, CH])

            for p in range(PAIRS):
                def wait(name):
                    dve.wait_ge(sem(name), p + 1)

                for i, dst in enumerate((R, K, V)):
                    shift(stages[f"rkv{p}"][0] + i, 3 + 3 * p + i, 8 * i + p, dst)
                do(V_.tensor_scalar(KK, K, prm("k_k", p), None, ALU.mult), "rw_kk")
                emptied(dve, "zw", p)
                do(V_.tensor_tensor_scan(CS, reset, SW, 0.0, ALU.mult, ALU.add))
                do(V_.tensor_tensor(WX, CS, SW, ALU.subtract), "rw_cs")
                made(dve, "ss", p)
                do(V_.tensor_scalar(DIFF, rbank("ss", p)[:], 1e-24, None, ALU.max), "rw_emptied_v")
                wait("rw_norm")
                do(V_.reciprocal(DIFF, DIFF))
                do(V_.tensor_tensor(KK, KK, DIFF, ALU.mult))
                emptied(dve, "za", p)
                do(V_.tensor_scalar(SW, A_, -1.0, prm("k_a", p), ALU.add, ALU.mult))
                do(V_.scalar_tensor_tensor(K, SW, 1.0, K, ALU.add, ALU.mult))
                do(V_.tensor_tensor(A_, A_, KK, ALU.mult))
                do(V_.scalar_tensor_tensor(RK, R, prm("r_k", p), K, ALU.mult, ALU.mult), "rw_rk")
                wait("rw_w")
                do(V_.scalar_tensor_tensor(AR[:, :, 0, :], by_chunk(KK), -1.0, by_chunk(WX), ALU.mult, ALU.mult))
                for h in range(2):
                    r, cols = slice(64 * h, 64 * h + 64), slice(64 * h, 64 * h + 64)
                    do(V_.tensor_tensor(BX[r, :, cols], by_chunk(A_)[r], by_chunk(WI)[r], ALU.mult))
                    do(V_.tensor_tensor(KX[r, :, cols], by_chunk(K)[r], by_chunk(WI)[r], ALU.mult))
                do(V_.tensor_tensor(AR[:, :, 1, :], by_chunk(R), by_chunk(W), ALU.mult), "rw_ar")
                made(dve, "bonus", p)
                do(V_.tensor_tensor(R, rbank("bonus", p)[:], V, ALU.mult), "rw_emptied_v")
                for h in range(2):
                    cs = slice(4 * h, 4 * h + 4)
                    for name, wide, narrow in ((f"bM{h}", LAB, RM[:, :, 0, :]), (f"kM{h}", LAK, MRK)):
                        made(dve, name, p)
                        src = four(rbank(name, p))
                        do(V_.tensor_tensor(both(wide[:, cs, :]), twice(src[:, :, 0:CH]), mask2(strict), ALU.mult))
                        do(V_.tensor_tensor(narrow[:, cs, :], src[:, :, CH:P], mask1(incl), ALU.mult), "rw_emptied_v")
                for h in range(2):
                    cs = slice(4 * h, 4 * h + 4)
                    do(V_.tensor_tensor(both(TTX[:, cs, :]), both(LAB[:, cs, :]), twice(mask1(level[:, 0, :])), ALU.mult))
                    do(V_.tensor_tensor(TTX[:, cs, :], TTX[:, cs, :], ident.unsqueeze(1).to_broadcast([P, 4, P]),
                                        ALU.add), "rw_tt0")
                for l in range(1, 6):
                    for h in range(2):
                        cs = slice(4 * h, 4 * h + 4)
                        made(dve, f"P{l}{h}", p)
                        do(V_.tensor_tensor(both(PX[:, cs, :]), both(four(rbank(f"P{l}{h}", p))),
                                            twice(mask1(level[:, l, :])), ALU.mult), "rw_emptied_v")
                    for h in range(2):
                        cs = slice(4 * h, 4 * h + 4)
                        made(dve, f"D{l}{h}", p)
                        do(V_.tensor_tensor(TX[:, cs, :], TX[:, cs, :], four(rbank(f"D{l}{h}", p)), ALU.add),
                           "rw_emptied_v")
                for h in range(2):
                    cs = slice(4 * h, 4 * h + 4)
                    made(dve, f"TAX{h}", p)
                    src = four(rbank(f"TAX{h}", p))
                    do(V_.tensor_tensor(both(TAX[:, cs, :]), twice(src[:, :, 0:CH]), mask2(heads), ALU.mult))
                    do(V_.tensor_tensor(both(X0X[:, cs, :]), twice(src[:, :, CH:P]), mask2(heads), ALU.mult))
                    do(V_.tensor_copy(X0C[:, cs, :], src[:, :, CH:P]), "rw_emptied_v")
                for h in range(2):
                    cs = slice(4 * h, 4 * h + 4)
                    made(dve, f"RM{h}", p)
                    src = four(rbank(f"RM{h}", p))
                    do(V_.tensor_tensor(AR[:, cs, 1, :], AR[:, cs, 1, :], src[:, :, 0:CH], ALU.add))
                    do(V_.tensor_tensor(both(MCX[:, cs, :]), twice(src[:, :, CH:P]), mask2(heads), ALU.mult))
                    do(V_.tensor_tensor(MCX[:, cs, :], MCX[:, cs, :], ident.unsqueeze(1).to_broadcast([P, 4, P]),
                                        ALU.add), "rw_emptied_v")
                w_end = by_chunk(W)[:, :, CH - 1:CH]
                for h in range(2):
                    cs = slice(4 * h, 4 * h + 4)
                    made(dve, f"N{h}", p)
                    do(V_.tensor_tensor(NP_[:, cs, :], rbank(f"N{h}", p)[:, 0:256].rearrange("p (c s) -> p c s", s=CH),
                                        w_end[:, cs, :].to_broadcast([P, 4, CH]), ALU.mult), "rw_emptied_v")
                do(V_.tensor_copy(SC_[:, 1, :], NP_[:, 0, :]), "rw_state")
                for c in range(1, NC - 1):
                    last = c == NC - 2
                    if last:
                        made(dve, "scan", p)
                    else:
                        dve.wait_ge(sem("rw_stepped"), p * (NC - 3) + c)
                    do(V_.scalar_tensor_tensor(SC_[:, c + 1, :], rbank("scan", p)[:, CH * c:CH * (c + 1)], w_end[:, c, :],
                                               NP_[:, c, :], ALU.mult, ALU.add),
                       "rw_emptied_v" if last else "rw_state")
                for h in range(2):
                    cs = slice(4 * h, 4 * h + 4)
                    if h == 0:
                        do(V_.memset(SC_[:, 0, :], 0.0))
                    do(V_.tensor_tensor(both(SX[:, cs, :]), twice(SC_[:, cs, :]), mask2(heads), ALU.mult),
                       "rw_sx" if h else "vector_step")
                made(dve, "mean", p)
                do(V_.scalar_tensor_tensor(YC, rbank("mean", p)[:], -1.0 / CH, K, ALU.mult, ALU.add), "rw_emptied_v")
                made(dve, "var", p)
                do(V_.tensor_scalar(WI, rbank("var", p)[:], 1.0 / CH, GN_EPS, ALU.mult, ALU.add), "rw_emptied_v")
                wait("rw_std")
                do(V_.reciprocal(WI, WI))
                do(V_.tensor_tensor(YC, YC, WI, ALU.mult))
                do(V_.tensor_scalar(YC, YC, prm("gn_w", p), prm("gn_b", p), ALU.mult, ALU.add))
                do(V_.tensor_tensor(YC, YC, R, ALU.add))
                q = splits["y_rwkv"][0] + p
                do(V_.tensor_tensor(tmp[:, q % 2, :], YC, G, ALU.mult), "tmp_ready")
                low(q)

            for t in range(*stages["attn_out"]):
                take_tile(t, lambda b, j=t - stages["attn_out"][0]: V_.tensor_copy(MERGED[:, j, :], b[:]))

            def gate():
                i = counts["gates"] = counts.get("gates", -1) + 1
                return gate_buf[:, i % 2, :]

            for j, t in enumerate(range(*stages["gate_a"])):
                evacuated(dve, t)
                do(V_.tensor_tensor(MERGED[:, j, :], MERGED[:, j, :], gate(), ALU.mult), "gate_used")

            def gated_pairs(name, first):
                t0, t1 = stages[name]
                for j in range(KT):
                    g = gate()
                    evacuated(dve, t0 + 2 * j)
                    dst = MERGED[:, j, :] if first else g
                    take_tile(t0 + 2 * j + 1, lambda b: V_.tensor_tensor(dst, g, b[:], ALU.mult))
                    if first:
                        do(V_.memset(small[:, 4 * ADA - 1:4 * ADA], 0.0), "gate_used")
                    else:
                        do(V_.tensor_tensor(MERGED[:, j, :], MERGED[:, j, :], g, ALU.add), "gate_used")

            gated_pairs("rwkv_out", False)
            split_all("merged", lambda j, d: do(V_.tensor_copy(d, MERGED[:, j, :]), "tmp_ready"))
            dve.wait_ge(sem("ld_x"), 32)
            for j in range(KT):
                add_to_h(stages["mix_out"][0] + j, j)

            inverse_deviation("mem", M)
            split_all("n_mem", lambda j, d: scaled_by(d[:, 0:M], MEM[:, j, :], prm("g_mem", j), "tmp_ready", M))
            inverse_deviation("x")
            split_all("n_x", lambda j, d: scaled_by(d, H[:, j, :], prm("g_x", j), "tmp_ready"))
            for hd in range(XH):
                dve.wait_ge(sem("x_raw"), hd + 1)
                for c in range(TC):
                    do(V_.tensor_reduce(x_stat[:, c, 0:1], banks[4 + c // 2][:, M * (c % 2):M * (c % 2 + 1)], AX_X,
                                        ALU.max, negate=True), "x_max" if c == TC - 1 else "vector_step")
                dve.wait_ge(sem("x_scored"), hd + 1)
                do(V_.reciprocal(x_stat[:, :, 2:3], x_stat[:, :, 1:2]))
                for c in range(TC):
                    do(V_.tensor_scalar(XP[:, c, :], XP[:, c, :], x_stat[:, c, 2:3], None, ALU.mult),
                       "x_p" if c == TC - 1 else "vector_step")
                dve.wait_ge(sem("x_y"), hd + 1)
                for d in range(2):
                    q = splits["x_o"][0] + 2 * hd + d
                    do(V_.tensor_copy(tmp[:, q % 2, :], banks[6 + d][:]), "tmp_ready")
                for d in range(2):
                    low(splits["x_o"][0] + 2 * hd + d)
            do(V_.memset(small[:, 4 * ADA - 1:4 * ADA], 0.0), "mem_done")
            for j in range(KT):
                add_to_h(stages["x_out"][0] + j, j)

            inverse_deviation("ffn")
            split_all("n_ffn", lambda j, d: scaled_by(d, H[:, j, :], prm("g_ffn", j), "tmp_ready"))
            for c, _ in enumerate(chunks_of(FF1)):
                t0 = stages[f"up{c}"][0]

                def squared(j, d):
                    evacuated(dve, t0 + j)
                    r = RELU[:, j % 2, :]
                    do(V_.tensor_tensor(d, r, r, ALU.mult), "tmp_ready")

                split_all(f"hidden{c}", squared)
                for j in range(KT):
                    add_to_h(stages[f"down{c}"][0] + j, j)
            dve.wait_ge(sem("ada_used"), 2 * ADA)
            for l in range(LAYERS):
                do(V_.tensor_tensor(mods[:, ADA * l:ADA * (l + 1)], banks[5][:, ADA * l:ADA * (l + 1)],
                                    prm(f"ada_b{l}", 0, ADA), ALU.add))
                for i in range(2):
                    do(V_.scalar_tensor_tensor(scaled[:, 16 * l + 8 * i:16 * l + 8 * i + 8],
                                               mods[:, ADA * l + 24 * i + 8:ADA * l + 24 * i + 16], 1.0,
                                               prm(f"norm{i + 1}_{l}", 0, 8), ALU.add, ALU.mult))
            inverse_deviation("final")
            for j in range(KT):
                scaled_by(H[:, j, :], H[:, j, :], prm("g_final", j), "final_done")

            for l in range(LAYERS):
                def mod(which, j):
                    return mods[:, ADA * l + 8 * which + j:ADA * l + 8 * which + j + 1]

                def modulated(i):
                    def op(j, d):
                        g = scaled[:, 16 * l + 8 * i + j:16 * l + 8 * i + j + 1]
                        do(V_.scalar_tensor_tensor(d, H[:, j, :], g, rstd[:], ALU.mult, ALU.mult))
                        do(V_.tensor_scalar(d, d, mod(3 * i, j), None, ALU.add), "tmp_ready")
                    return op

                inverse_deviation(f"n1_{l}")
                split_all(f"n1_{l}", modulated(0))

                def fourier(j, d):
                    dve.wait_ge(sem("f_made"), KT * l + j + 1)
                    do(V_.tensor_copy(d, banks[6 + j % 2][:]), "tmp_ready")

                split_all(f"fourier{l}", fourier)
                gated_pairs(f"fourier_out{l}", True)
                for hd in range(XH):
                    n = XH * l + hd
                    if hd == 0:
                        dve.wait_ge(sem("ret_tables"), 32 * (l + 1))
                    for what, dst in (("q", RQ), ("k", RKY)):
                        t0 = stages[f"ret_{what}{l}_{hd}"][0]
                        b0, b1 = banks[t0 % BANKS], banks[(t0 + 1) % BANKS]
                        tile_done(dve, t0 + 1)
                        do(V_.tensor_tensor(ROT[:, 0, :], b0[:], COS, ALU.mult))
                        do(V_.tensor_tensor(ROT[:, 1, :], b1[:], SIN, ALU.mult))
                        do(V_.tensor_tensor(dst[:, 0, :], ROT[:, 0, :], ROT[:, 1, :], ALU.subtract))
                        take_tile(t0, lambda b: V_.tensor_tensor(ROT[:, 0, :], b[:], SIN, ALU.mult))
                        take_tile(t0 + 1, lambda b: V_.tensor_tensor(ROT[:, 1, :], b[:], COS, ALU.mult))
                        do(V_.tensor_tensor(dst[:, 1, :], ROT[:, 0, :], ROT[:, 1, :], ALU.add), "rotated")
                    dve.wait_ge(sem("strip_landed"), 16 * (n + 1))
                    for c in range(TC):
                        dve.wait_ge(sem("ret_raw"), TC * n + c + 1)
                        do(V_.tensor_tensor(RP[:, c, :], banks[4 + c % 2][:], STRIP[:, 384 - P * c:896 - P * c],
                                            ALU.mult), "ret_masked")
                    dve.wait_ge(sem("ret_mean"), n + 1)
                    for d in range(2):
                        do(V_.scalar_tensor_tensor(RY[:, d, :], banks[6][:], -1.0 / 256, RY[:, d, :], ALU.mult,
                                                   ALU.add), "ret_centred")
                    dve.wait_ge(sem("ret_var"), n + 1)
                    do(V_.tensor_scalar(ROT[:, 0, :], banks[7][:], 1.0 / 256, EPS, ALU.mult, ALU.add), "ret_var_read")
                    dve.wait_ge(sem("ret_std"), n + 1)
                    do(V_.reciprocal(ROT[:, 0, :], ROT[:, 0, :]))
                    for t in range(*stages[f"ret_g{l}_{hd}"]):
                        evacuated(dve, t)
                    for d in range(2):
                        q = splits[f"ret{l}"][0] + 2 * hd + d
                        do(V_.tensor_tensor(RY[:, d, :], RY[:, d, :], ROT[:, 0, :], ALU.mult))
                        do(V_.tensor_tensor(tmp[:, q % 2, :], RY[:, d, :], RG[:, d, :], ALU.mult), "tmp_ready")
                    for d in range(2):
                        low(splits[f"ret{l}"][0] + 2 * hd + d)
                gated_pairs(f"ret_out{l}", False)
                split_all(f"m{l}", lambda j, d: do(V_.tensor_copy(d, MERGED[:, j, :]), "tmp_ready"))
                for j in range(KT):
                    add_to_h(stages[f"out{l}"][0] + j, j, mod(2, j))
                inverse_deviation(f"n2_{l}")
                split_all(f"n2_{l}", modulated(1))
                do(V_.memset(FRAW[:, :, 0:8], 0.0))
                do(V_.memset(FRAW[:, :, 520:528], 0.0))
                for c, (a, n_hidden) in enumerate(chunks_of(FF2)):
                    t0 = stages[f"ff_in{l}_{c}"][0]

                    def gated(j, d):
                        i = FF2 * l + a + j
                        for half in range(2):
                            evacuated(dve, t0 + 2 * j + half)
                            raw, o, col = FRAW[:, half, :], CONV[:, i % 2, half, :], FF2 * half + a + j
                            do(V_.tensor_scalar(o, raw[:, 7:7 + S], prm(f"conv0_{l}", col), prm(f"conv_b{l}", col),
                                                ALU.mult, ALU.add))
                            do(V_.scalar_tensor_tensor(o, raw[:, 8:8 + S], prm(f"conv1_{l}", col), o, ALU.mult, ALU.add))
                            do(V_.scalar_tensor_tensor(o, raw[:, 9:9 + S], prm(f"conv2_{l}", col), o, ALU.mult, ALU.add),
                               "conv_done")
                        dve.wait_ge(sem("gelu"), i + 1)
                        do(V_.tensor_tensor(d, CONV[:, i % 2, 0, :], CONV[:, i % 2, 1, :], ALU.mult), "tmp_ready")

                    split_all(f"ff{l}_{c}", gated)
                    for j in range(KT):
                        add_to_h(stages[f"ff_out{l}_{c}"][0] + j, j, mod(5, j))
            inverse_deviation("out")
            for j in range(KT):
                scaled_by(H[:, j, :], H[:, j, :], prm("g_out", j), "y_done")


def constant_arrays():
    f = np.float32
    i = np.arange(P)
    tables = {}
    head, pos = i // CH, i % CH
    same = head[:, None] == head[None, :]
    tables["ident"] = np.eye(P)
    tables["ones"] = np.ones((P, P))
    tables["heads"] = same
    tables["strict"] = same & (pos[:, None] < pos[None, :])
    s = np.arange(CH)
    tables["incl"] = pos[:, None] <= s[None, :]
    levels = [(pos[:, None] // 2 == s[None, :] // 2) & (pos[:, None] < s[None, :])]
    for l in range(1, 6):
        b = 2 ** l
        levels.append((pos[:, None] // (2 * b) == s[None, :] // (2 * b)) & (pos[:, None] % (2 * b) >= b)
                      & (s[None, :] % (2 * b) < b))
    tables["level"] = np.concatenate(levels, 1)
    tables["ident_c"] = pos[:, None] == s[None, :]
    tables["reset"] = np.broadcast_to(np.arange(S) % CH != 0, (P, S))
    table = np.concatenate([np.asarray(tables[n], f) for n, _ in TABLE], 1)

    far = 1e30
    steps = i[:, None] + P - np.arange(2 * P)[None, :]
    dist = [np.where((steps >= 0) & (steps <= P), steps, far)]
    steps = i[:, None] + 3 * P - np.arange(4 * P)[None, :]
    for dilation in (4, 16):
        dist.append(np.where((steps >= 0) & (steps % dilation == 0), steps, far))
    dist = np.concatenate(dist, 1).astype(f)

    a = 2 * np.pi * (np.outer(np.arange(S), np.arange(S)) % S) / S
    dft_cos = (np.cos(a) / np.sqrt(S)).astype(f).reshape(TC, P, S).transpose(1, 0, 2)
    dft_sin = (-np.sin(a) / np.sqrt(S)).astype(f).reshape(TC, P, S).transpose(1, 0, 2)
    a = 2 * np.pi * (np.outer(i, i) % P) / P
    dft_feature = (np.concatenate([np.cos(a), np.sin(a)], 1) / np.sqrt(P)).astype(f)

    inv_freq = (f(10000.0) ** (-i.astype(f) / f(P))).astype(f)
    angle = (inv_freq[:, None] * np.arange(S, dtype=f)[None, :]).astype(f).astype(np.float64)
    rotary = np.stack([np.cos(angle), np.sin(angle)], 1).astype(f)

    strips = []
    d = np.arange(896)[None, :] - 384 - i[:, None]
    for h in range(XH):
        fwd, bwd = np.log1p(-2.0 ** (-5.0 - h)), np.log1p(-2.0 ** (-5.5 - h))
        strips.append(np.exp(np.where(d >= 0, fwd * d, -bwd * d)) / 16)
    return dict(table=table, dist=dist, dft_cos=dft_cos, dft_sin=dft_sin, dft_feature=dft_feature, rotary=rotary,
                strips=np.stack(strips).astype(f))


def feature_major(a):
    return a.T.reshape(-1, P, a.shape[0]).transpose(1, 0, 2)


def pad_to(a, n):
    out = np.zeros(a.shape[:-1] + (n,), a.dtype)
    out[..., :a.shape[-1]] = a
    return out


def lay_out(inputs, plan):
    x = {k: np.asarray(v) for k, v in inputs.items()}
    w_in = x["w_in"]
    names = dict(x)
    names["w_in_lora"] = pad_to(w_in[:, :, 3072:3360], 384)
    order = np.concatenate([np.arange(P) + 1024 * s + P * p for p in range(PAIRS) for s in range(3)])
    names["w_in_pair"] = w_in[:, :, order]
    f = np.float32
    weights = np.zeros((len(plan.source), P, UNIT), f)
    for u, src in enumerate(plan.source):
        if src[0] == "blocks":
            _, name, layer, row, col, k, b0, n = src
            w = names[name][layer]
            for b in range(n):
                j, i = divmod(b0 + b, k)
                weights[u, :, P * b:P * (b + 1)] = w[row + P * i:row + P * (i + 1), col + P * j:col + P * (j + 1)]
        elif src[0] == "rows":
            _, name, layer, row, col, w, per = src
            m = names[name][layer]
            for b in range(per):
                weights[u, :, w * b:w * (b + 1)] = m[row + P * b:row + P * (b + 1), col:col + w]
    ada = x["ada_w_2"].reshape(LAYERS, KT, P, ADA, P).transpose(0, 3, 2, 1, 4).reshape(LAYERS * ADA, P, UNIT)
    w2, a2, g2 = x["w2"][0], x["a2"][0], x["g2"][0]
    lora = np.zeros((PAIRS, P, 4, P), f)
    for p in range(PAIRS):
        c = slice(P * p, P * (p + 1))
        lora[p, 0:64, 0], lora[p, 64:128, 0] = w2[:, c], a2[:, c]
        lora[p, :, 1], lora[p, 0:32, 2] = g2[0:128, c], g2[128:160, c]
    vec = {"g_mix": x["norm_mix_g"], "mu": pad_to(x["shift_mu"], 27 * P), "w0": x["w0"], "a0": x["a0"],
           "k_k": x["k_k"], "k_a": x["k_a"], "r_k": x["r_k"], "gn_w": x["gn_w"], "gn_b": x["gn_b"],
           "g_x": x["norm_x_g"], "g_mem": x["norm_mem_g"], "g_ffn": x["norm_ffn_g"], "g_final": x["norm_final_g"],
           "c": x["c_2"], "g_out": x["final_g_2"]}
    for l in range(LAYERS):
        vec[f"norm1_{l}"], vec[f"norm2_{l}"] = x["norm1_g_2"][l], x["norm2_g_2"][l]
        vec[f"ada_b{l}"], vec[f"conv_b{l}"] = x["ada_b_2"][l], x["conv_b_2"][l]
        for i in range(3):
            vec[f"conv{i}_{l}"] = x["conv_w_2"][l, i]
    params = np.concatenate([vec[n].reshape(-1, P).T for n, _ in PARAMS], 1)
    arrays = dict(weights=weights, ada=ada, lora_w=lora, params=params, x=feature_major(x["x"][0]),
                  mem=feature_major(x["mem"][0]))
    arrays.update(constant_arrays())
    return {k: np.ascontiguousarray(v) for k, v in arrays.items()}


def kernel(**inputs):
    import concourse.bacc as bacc
    from concourse.bass_utils import run_bass_kernel_spmd

    plan = make_plan()
    arrays = lay_out(inputs, plan)
    nc = bacc.Bacc("TRN2", target_bir_lowering=False, num_devices=1, dynamic_dma_scratch_size=1024)
    aps = {k: nc.dram_tensor("in_" + k, a.shape, mybir.dt.from_np(a.dtype), kind="ExternalInput").ap()
           for k, a in arrays.items()}
    out = nc.dram_tensor("out_y", (P, KT, S), F32, kind="ExternalOutput").ap()
    build_program(nc, plan, aps, out)
    r = run_bass_kernel_spmd(nc, [{"in_" + k: a for k, a in arrays.items()}], core_ids=[0])
    y = np.asarray(r.results[0]["out_y"])
    return np.ascontiguousarray(y.transpose(2, 1, 0)).reshape(1, S, D)
```

```python
from contextlib import ExitStack

import numpy as np
import concourse.bass as bass
from concourse import mybir

P = 128
F32 = mybir.dt.float32
F32R = mybir.dt.float32r
ALU = mybir.AluOpType
ACT = mybir.ActivationFunctionType
AX_X = mybir.AxisListType.X

D = 1024
S = 512
M = 256
KT = D // P
TC = S // P
CH = 64
NC = S // CH
PAIRS = 8
AH = 12
XH = 4
FF1 = 4096 // P
FF2 = 2816 // P
LAYERS = 2
RING = 4
AHEAD = 2
BANKS = 4
ARENA = 21000
UNIT = 1024
ADA = 48
EPS = 1e-6
GN_EPS = 64 * 1e-5
LOG_DECAY = -float(np.exp(-0.5))


def columns(names):
    at, out = 0, {}
    for name, n in names:
        out[name] = (at, at + n)
        at += n
    return out, at


PARAMS = [("g_mix", 8), ("mu", 27), ("w0", 8), ("a0", 8), ("k_k", 8), ("k_a", 8), ("r_k", 8), ("gn_w", 8),
          ("gn_b", 8), ("g_x", 8), ("g_mem", 8), ("g_ffn", 8), ("g_final", 8), ("c", 8), ("g_out", 8)]
for _l in range(LAYERS):
    PARAMS += [(f"norm1_{_l}", 8), (f"norm2_{_l}", 8), (f"ada_b{_l}", ADA)]
    PARAMS += [(f"conv{_i}_{_l}", 2 * FF2) for _i in range(3)] + [(f"conv_b{_l}", 2 * FF2)]
PCOL, PTOTAL = columns(PARAMS)

TABLE = [("ident", 128), ("ones", 128), ("heads", 128), ("strict", 128), ("incl", 64), ("level", 6 * 64),
         ("ident_c", 64), ("reset", 512)]
TCOL, TTOTAL = columns(TABLE)


def chunks_of(n, size=8):
    return [(a, min(size, n - a)) for a in range(0, n, size)]


class Plan:

    def __init__(self):
        self.tiles, self.stages, self.source, self.conv, self.splits = [], {}, [], [], {}

    def unit(self, *source):
        self.source.append(source)
        return len(self.source) - 1

    def plain(self, name, weight, layer, col, n, row=0, k=KT, src="A1"):
        start, per = len(self.tiles), UNIT // P
        for j in range(n):
            blocks = []
            for i in range(k):
                b = j * k + i
                if b % per == 0:
                    self.unit("blocks", weight, layer, row, col, k, b, min(per, n * k - b))
                blocks.append((len(self.source) - 1, P * (b % per), i))
            self.tiles.append(dict(blocks=blocks, src=src, rows=False))
        self.stages[name] = (start, len(self.tiles))

    def pairs(self, name, one, other, n):
        start = len(self.tiles)
        for j in range(n):
            for weight, layer, col, src in (one, other):
                u = self.unit("blocks", weight, layer, 0, col + P * j, KT, 0, KT)
                self.tiles.append(dict(blocks=[(u, P * i, i) for i in range(KT)], src=src, rows=False))
        self.stages[name] = (start, len(self.tiles))

    def token_major(self, name, weight, layer, col, cols, token_tiles, src="A1"):
        start = len(self.tiles)
        for c0 in range(0, cols, 512):
            w = min(512, cols - c0)
            per = UNIT // w
            us = [self.unit("rows", weight, layer, per * P * q, col + c0, w, per) for q in range(KT // per)]
            for t in range(token_tiles):
                self.tiles.append(dict(blocks=[(us[i // per], w * (i % per), i) for i in range(KT)], src=src,
                                       rows=True, width=w, token=t, col=c0))
        self.stages[name] = (start, len(self.tiles))

    def split(self, name, buf, n, free_after):
        self.splits[name] = (len(self.conv), len(self.conv) + n)
        for j in range(n):
            self.conv.append((buf, j, self.stages[free_after][1] if free_after else 0))


def make_plan():
    p = Plan()
    p.split("n_mix", "A1", 8, None)
    p.plain("qk", "w_in", 0, 3360, 12)
    p.token_major("v", "w_in", 0, 3360 + 1536, 768, TC)
    p.split("y_attn", "YA", 2, None)
    p.plain("lora", "w_in_lora", 0, 0, 3)
    for q in range(PAIRS):
        p.plain(f"rkv{q}", "w_in_pair", 0, 384 * q, 3)
    p.split("y_rwkv", "A2", 8, None)
    p.plain("gate_a", "w_in", 0, 3360 + 2304 + 1024, 8)
    p.plain("attn_out", "p_attn", 0, 0, 8, k=2, src="YA")
    p.pairs("rwkv_out", ("w_in", 0, 3360 + 2304, "A1"), ("p_rwkv", 0, 0, "A2"), 8)
    p.split("merged", "A1", 8, "rwkv_out")
    p.plain("mix_out", "w_out", 0, 0, 8)
    p.split("n_mem", "A2", 8, "rwkv_out")
    p.plain("mem_k", "xa_wkv", 0, 0, 8, src="A2")
    p.token_major("mem_v", "xa_wkv", 0, 1024, 1024, 2, src="A2")
    p.split("n_x", "A1", 8, "mix_out")
    p.plain("x_q", "xa_wq", 0, 0, 8)
    p.split("x_o", "A2", 8, "mem_v")
    p.plain("x_out", "xa_wo", 0, 0, 8, src="A2")
    p.split("n_ffn", "A1", 8, "x_q")
    before = "x_out"
    for c, (a, n) in enumerate(chunks_of(FF1)):
        p.plain(f"up{c}", "ffn_w1", 0, P * a, n)
        p.split(f"hidden{c}", "A2", n, before)
        p.plain(f"down{c}", "ffn_w2", 0, 0, 8, row=P * a, k=n, src="A2")
        before = f"down{c}"
    for l in range(LAYERS):
        p.split(f"n1_{l}", "A1", 8, "up3" if l == 0 else "ff_in0_2")
        p.plain(f"fourier_in{l}", "w_in_2", l, 0, 8)
        p.split(f"fourier{l}", "A2", 8, before)
        p.pairs(f"fourier_out{l}", ("w_in_2", l, 5120, "A1"), ("w_fourier_2", l, 0, "A2"), 8)
        for h in range(XH):
            p.plain(f"ret_q{l}_{h}", "w_in_2", l, 1024 + 256 * h, 2)
            p.plain(f"ret_k{l}_{h}", "w_in_2", l, 2048 + 256 * h, 2)
            p.token_major(f"ret_v{l}_{h}", "w_in_2", l, 3072 + 256 * h, 256, TC)
            p.plain(f"ret_g{l}_{h}", "w_in_2", l, 4096 + 256 * h, 2)
        p.split(f"ret{l}", "A2", 8, f"fourier_out{l}")
        p.pairs(f"ret_out{l}", ("w_in_2", l, 6144, "A1"), ("w_ret_2", l, 0, "A2"), 8)
        p.split(f"m{l}", "A1", 8, f"ret_out{l}")
        p.plain(f"out{l}", "w_out_2", l, 0, 8)
        p.split(f"n2_{l}", "A1", 8, f"out{l}")
        before = f"ret_out{l}"
        for c, (a, n) in enumerate(chunks_of(FF2)):
            p.pairs(f"ff_in{l}_{c}", ("ffn_up_2", l, P * a, "A1"), ("ffn_up_2", l, P * (FF2 + a), "A1"), n)
            p.split(f"ff{l}_{c}", "A2", n, before)
            p.plain(f"ff_out{l}_{c}", "ffn_down_2", l, 0, 8, row=P * a, k=n, src="A2")
            before = f"ff_out{l}_{c}"
    while len(p.source) % RING:
        p.unit("none")
    return p


def build_program(nc, plan, ap, out):
    tiles, stages, conv, splits = plan.tiles, plan.stages, plan.conv, plan.splits
    n_units = len(plan.source)
    last_tile = {}
    for t, T in enumerate(tiles):
        for u, _, _ in T["blocks"]:
            last_tile[u] = t

    ctx = ExitStack()
    with ctx:
        def sb(name, shape, dt=F32):
            return ctx.enter_context(nc.sbuf_tensor(name, shape, dt))

        sems = {}

        def sem(name):
            if name not in sems:
                sems[name] = ctx.enter_context(nc.semaphore(name))
            return sems[name]

        w_raw = sb("w_raw", [P, RING, UNIT])
        w_hi = sb("w_hi", [P, RING, UNIT], F32R)
        w_lo = sb("w_lo", [P, RING, UNIT], F32R)
        with nc.sbuf_tensor("arena2", [P, 2 * KT * S], F32) as arena2:
            pass
        acts = {"A2": sb("act2", [P, 2, KT, S], F32R), "A1": sb("act1", [P, 2, KT, S], F32R),
                "YA": sb("act_attn", [P, 2, 2, S], F32R)}
        params = sb("params", [P, PTOTAL])
        table = sb("table", [P, TTOTAL])
        tmp = sb("tmp", [P, 2, S])
        squares = sb("squares", [P, 2, S])
        rstd = sb("rstd", [P, S])
        small = sb("small", [P, 4 * ADA])
        stats = sb("stats", [P, 2, 8])
        exponent = sb("exponent", [P, 8])
        arena = sb("arena", [P, ARENA])
        banks = [ctx.enter_context(nc.psum_tensor(f"bank{i}", [P, 512], F32)) for i in range(8)]

        free_at = [0]

        def take(*shape):
            n = 1
            for x in shape:
                n *= x
            a = arena[:, free_at[0]:free_at[0] + n]
            free_at[0] += n
            assert free_at[0] <= ARENA, (free_at[0], ARENA)
            if len(shape) == 2:
                return a.rearrange("p (a b) -> p a b", b=shape[1])
            if len(shape) == 3:
                return a.rearrange("p (a b c) -> p a b c", b=shape[1], c=shape[2])
            return a

        def prm(name, j=0, n=1):
            return params[:, PCOL[name][0] + j:PCOL[name][0] + j + n]

        def tab(name):
            return table[:, TCOL[name][0]:TCOL[name][1]]

        ident, ones, heads, strict, incl, ident_c, reset = (
            tab(n) for n in ("ident", "ones", "heads", "strict", "incl", "ident_c", "reset"))
        level = tab("level").rearrange("p (l s) -> p l s", s=CH)

        H = take(KT, S)
        MERGED = take(KT, S)
        gate_buf = take(2, S)
        base = free_at[0]
        free_at[0] = KT * S
        QK = take(12, S)
        VT = take(TC, 768)
        SC = take(2, 1280)
        PT = take(1280)
        DIST = take(1280)
        att_stat = take(2, 4)
        free_at[0] = 0
        RAW = take(2, 520)
        LORA = take(S)
        GD = take(2, S)
        LW_DA, LW_G = take(P), take(2, P)
        R, K, V, SW, W, WI, WX, A_, KK, YC, BO0 = (take(S) for _ in range(11))
        DIFF, RK, CS = rstd[:], squares[:, 0, :], squares[:, 1, :]
        AR0 = take(NC, 2, CH)
        GATES_AT = free_at[0]
        BX0, KX0, VX0, AX0, LAB, LAK, TX, TTX = (take(NC, P) for _ in range(8))
        RM = take(NC, 2, CH)
        MRK = take(NC, CH)
        VC = take(NC, CH)
        AZ = take(NC, 2, CH)
        main_end, main_arena = free_at[0], arena
        arena, free_at[0] = arena2, 0
        AR1 = take(NC, 2, CH)
        BX1, KX1, VX1, AX1 = (take(NC, P) for _ in range(4))
        X0C, NP_, SC_ = (take(NC, CH) for _ in range(3))
        YK, YSQ, BO1 = (take(S) for _ in range(3))
        arena = main_arena
        ARs, BXs, KXs, VXs, AXs, BOs = (AR0, AR1), (BX0, BX1), (KX0, KX1), (VX0, VX1), (AX0, AX1), (BO0, BO1)
        X0X, MCX, SX = LAK, TX, LAB
        YO = tmp
        free_at[0] = GATES_AT
        GATES = take(KT, S)
        YB = take(KT, S)
        MEM = take(KT, M)
        free_at[0] = base
        KM = MERGED[:, 0:4, :].rearrange("p a (b m) -> p (a b) m", m=M)
        VM = MERGED[:, 4:8, :].rearrange("p (a b) m -> p a (b m)", a=2)
        XQ = YB
        XP = take(TC, M)
        XPT = take(2, S)
        x_stat = take(TC, 4)
        assert free_at[0] <= GATES_AT + KT * S
        free_at[0] = base
        ADA_W = take(4, UNIT)
        ADA_SUM = take(ADA * P)
        RELU = take(2, S)
        free_at[0] = base
        CS_SEQ = take(TC, S)
        SN_SEQ = take(TC, S)
        CS_FEAT = take(256)
        UF = take(2, S)
        PF = take(2, TC, 256)
        free_at[0] = base
        COS = take(S)
        SIN = take(S)
        RQ = take(2, S)
        RKY = take(2, S)
        ROT = take(4, S)
        RV = take(TC, 256)
        STRIP = take(896)
        RP = take(TC, S)
        RG = take(2, S)
        RY = take(2, S)
        free_at[0] = base
        FRAW = take(2, 528)
        CONV = take(2, 2, S)

        y_scratch = nc.dram_tensor("y_scratch", (PAIRS - 1, P, S), F32).ap()
        mods = small[:, 0:2 * ADA]
        scaled = small[:, 2 * ADA:2 * ADA + 32]
        c_act = small[:, 2 * ADA + 32:2 * ADA + 40]
        half_bias = small[:, 2 * ADA + 40:2 * ADA + 56]
        w_ends = small[:, 2 * ADA + 56:2 * ADA + 72].rearrange("p (a c) -> p a c", a=2)
        spare = small[:, 4 * ADA - 1:4 * ADA]
        ADA_SPAN = 2 * FF1 - KT

        def ada_units(i):
            return range(2 * ADA * i // ADA_SPAN, 2 * ADA * (i + 1) // ADA_SPAN)


        block = ctx.enter_context(nc.Block())

        def evacuated(eng, t):
            eng.wait_ge(sem(f"bank_free{t % BANKS}"), t // BANKS + 1)

        def all_evacuated(eng, stage):
            end = stages[stage][1]
            for t in range(end - BANKS, end):
                evacuated(eng, t)

        def tile_done(eng, t):
            eng.wait_ge(sem("tile_done"), t + 1)

        STEPS = []
        STEPS += [(name, "v") for name in ("bM0", "bM1", "kM0", "kM1")]
        for h in range(2):
            STEPS += [(f"tT{h}", "a"), (f"tA{h}", "a")]
        for l in range(1, 6):
            for what in ("P", "D", "X"):
                for h in range(2):
                    STEPS += [(f"{what}{l}{h}", "a" if what == "X" else "v")]
                h = "PD".find(what)
                if l == 1 and h >= 0:
                    STEPS += [(f"tB{h}", "a"), (f"tV{h}", "a")]
            if l == 1:
                STEPS += [("tK0", "a"), ("tK1", "a"), ("Z0", "a"), ("Z1", "a")]
        STEPS += [(f"{w}{h}", "v") for w in ("TAX", "RM", "N") for h in range(2)]
        STEPS += [("scan", "v"), ("Y", "a")]
        INDEX = {name: n for n, (name, _) in enumerate(STEPS)}
        EVACS = {e: sum(1 for _, x in STEPS if x == e) for e in "av"}

        def emptied(eng, name, p):
            n = INDEX[name]
            e = STEPS[n][1]
            eng.wait_ge(sem("rw_emptied_" + e), p * EVACS[e] + sum(1 for _, x in STEPS[:n + 1] if x == e))

        def made(eng, name, p):
            eng.wait_ge(sem("rw_made"), p * len(STEPS) + INDEX[name] + 1)

        def rbank(name, p):
            return banks[5 + (p * len(STEPS) + INDEX[name]) % 3]

        SIDE = [(n, 0) for n in ("zw", "za", "ks", "kb", "bo")]
        for p in range(PAIRS + 1):
            for n in ("mn", "zw", "vs", "za", "vb", "ks", "zg", "kb", "bo"):
                q = p - 1 if n in ("mn", "vs", "vb", "zg") else p + 1
                if 0 <= q < PAIRS and (p, q) != (PAIRS, PAIRS):
                    SIDE.append((n, q))
        SIDE_AT = {}
        for n, key in enumerate(SIDE):
            SIDE_AT[key] = n

        def side_free(eng, name, p):
            if SIDE_AT[name, p]:
                eng.wait_ge(sem("side_emptied"), SIDE_AT[name, p])

        def side_made(eng, name, p):
            eng.wait_ge(sem("side_made"), sum(1 for n, _ in SIDE[:SIDE_AT[name, p] + 1] if n not in ("kb", "vb")))

        def rsqrt(n):
            return stats[:, n % 2, :]

        def beside(p):
            if p + 2 < PAIRS:
                return list(range(*stages[f"rkv{p + 2}"]))
            t = stages["gate_a"][0] + 4 * (p + 2 - PAIRS)
            return list(range(t, t + 4))

        NORMS = ["mix", "mem", "x", "ffn", "final"] + [f"{w}_{l}" for l in range(LAYERS) for w in ("n1", "n2")] + ["out"]

        def squares_before(name):
            return 8 * NORMS.index(name)

        REQUESTS = [(None, TC)]
        REQUESTS += [(stages["rkv0"][1] - 1, 2 * TC)]
        for p in range(PAIRS):
            last = stages[f"rkv{p + 1}"][1] - 1 if p + 1 < PAIRS else stages["gate_a"][0] + 3
            REQUESTS += [(last, 2 * TC)] * ((p > 0) + (p + 1 < PAIRS))
        REQUESTS += [(stages["gate_a"][1] - 1, 2 * TC)]
        REQUESTS += [(stages["mix_out"][0] + 4, M // P), (stages["mem_k"][1] - 1, TC), (stages["x_out"][1] - 1, TC),
                     (stages[f"down{len(chunks_of(FF1)) - 1}"][1] - 1, TC)]
        for l in range(LAYERS):
            before = f"down{len(chunks_of(FF1)) - 1}" if l == 0 else f"ff_out{l - 1}_{len(chunks_of(FF2)) - 1}"
            REQUESTS += [(stages[before][1] - 1, TC)]
            for hd in range(XH):
                before = f"ret_k{l}_{hd + 1}" if hd + 1 < XH else f"ret_g{l}_{hd}"
                REQUESTS += [(stages[before][1] - 1, TC)]
            REQUESTS += [(stages[f"out{l}"][1] - 1, TC)]
        REQUESTS += [(len(tiles) - 1, TC)]

        @block.sync
        def _(sp):
            first_up = min(u for u, _, _ in tiles[stages["up0"][0]]["blocks"])
            for u in range(n_units):
                k = u % RING
                n = u - first_up - AHEAD - 1
                for i in (ada_units(n) if 0 <= n < ADA_SPAN else ()):
                    if i == 0:
                        sp.wait_ge(sem("x_done"), 1)
                    if i >= 4:
                        sp.wait_ge(sem("ada_used"), i - 3)
                    sp.dma_start(ADA_W[:, i % 4, :], ap["ada"][i]).then_inc(sem(f"ada_landed{i % 4}"), 16)
                if u >= RING:
                    sp.wait_ge(sem("w_low"), u - RING + 1)
                sp.dma_start(w_raw[:, k, :], ap["weights"][u]).then_inc(sem(f"w_landed{k}"), 16)
            sp.wait_ge(sem("y_done"), KT)
            sp.dma_start(out, H).then_inc(sem("stored"), 16)
            sp.wait_ge(sem("stored"), 16)

        @block.gpsimd
        def _(pool):
            done = [0]

            def low_weights(end):
                for u in range(done[0], min(end, n_units)):
                    k = u % RING
                    pool.wait_ge(sem("w_high"), u + 1)
                    if u >= RING:
                        pool.wait_ge(sem("tile_done"), last_tile[u - RING] + 1)
                    nc.gpsimd.tensor_tensor(w_lo[:, k, :], w_raw[:, k, :], w_hi[:, k, :].bitcast(F32),
                                            ALU.subtract).then_inc(sem("w_low"), 1)
                done[0] = max(done[0], min(end, n_units))

            nc.gpsimd.memset(exponent[:], -0.5).then_inc(sem("exponent_set"), 1)
            pool.wait_ge(sem("exponent_set"), 1)
            for r, (t, cols) in enumerate(REQUESTS):
                low_weights(max(u for u, _, _ in tiles[t]["blocks"]) + 1 + AHEAD if t is not None else AHEAD)
                pool.wait_ge(sem("stats_ready"), r + 1)
                if r >= 2:
                    pool.wait_ge(sem("spread"), r - 1)
                x = rsqrt(r)[:, 0:cols]
                nc.gpsimd.tensor_tensor(x, x, exponent[:, 0:cols], ALU.pow).then_inc(sem("inverse_ready"), 1)
            low_weights(n_units)

        @block.tensor
        def _(pe):
            seen = {"low": 0, "weights": 0}

            def tile(t, first_conv, n=S, only=None):
                T = tiles[t]
                if t >= BANKS and not only:
                    evacuated(pe, t - BANKS)
                src = acts[T["src"]]
                dst = banks[t % BANKS]
                for i, (u, col, k) in enumerate(T["blocks"]):
                    if only is not None and i != only:
                        continue
                    if u + 1 > seen["weights"]:
                        pe.wait_ge(sem("w_low"), u + 1)
                        seen["weights"] = u + 1
                    if first_conv + k + 1 > seen["low"]:
                        pe.wait_ge(sem("low_done"), first_conv + k + 1)
                        seen["low"] = first_conv + k + 1
                    s = u % RING
                    first, last = i == 0, i == len(T["blocks"]) - 1
                    if T["rows"]:
                        w = T["width"]
                        xs = [src[:, q, k, T["token"] * P:(T["token"] + 1) * P] for q in range(2)]
                        wh, wl = w_hi[:, s, col:col + w], w_lo[:, s, col:col + w]
                        o = dst[:, 0:w]
                        nc.tensor.matmul(o, xs[0], wh, start=first, stop=False)
                        nc.tensor.matmul(o, xs[0], wl, start=False, stop=False)
                        mm = nc.tensor.matmul(o, xs[1], wh, start=False, stop=last)
                    else:
                        wh, wl = w_hi[:, s, col:col + P], w_lo[:, s, col:col + P]
                        xh, xl = src[:, 0, k, 0:n], src[:, 1, k, 0:n]
                        o = dst[:, 0:n]
                        nc.tensor.matmul(o, wh, xh, start=first, stop=False)
                        nc.tensor.matmul(o, wh, xl, start=False, stop=False)
                        mm = nc.tensor.matmul(o, wl, xh, start=False, stop=last)
                if last:
                    mm.then_inc(sem("tile_done"), 1)

            requests = [0]

            def sum_squares(name, j, n=S):
                s = squares_before(name) + j
                pe.wait_ge(sem("sq_ready"), s + 1)
                if j == 0 and NORMS.index(name):
                    pe.wait_ge(sem("stats_ready"), requests[0])
                for c in range(n // P):
                    mm = nc.tensor.matmul(banks[5][:, c:c + 1], squares[:, s % 2, c * P:(c + 1) * P], ones[:, 0:1],
                                          start=(j == 0 and c == 0), stop=(j == KT - 1), skip_group_check=True)
                mm.then_inc(sem("sq_used"), 1)

            def spread(bank, n=S, per=1):
                r = requests[0]
                requests[0] += 1
                pe.wait_ge(sem("inverse_ready"), r + 1)
                for c in range(n // P):
                    for i in range(per):
                        w = P // per
                        mm = nc.tensor.matmul(bank[w * i:w * (i + 1), c * P:(c + 1) * P],
                                              rsqrt(r)[:, per * c + i:per * c + i + 1].to_broadcast([P, w]), ident,
                                              start=True, stop=True)
                mm.then_inc(sem("spread"), 1)

            def stage(name, split, n=S, norm=None):
                t0, t1 = stages[name]
                for t in range(t0, t1):
                    tile(t, splits[split][0], n)
                    if norm and t > t0:
                        sum_squares(norm, t - t0 - 1)
                if norm:
                    sum_squares(norm, KT - 1)
                    spread(banks[4])

            def pair_stage(name, one, other, done=0):
                t0, t1 = stages[name]
                for t in range(t0 + done, t1):
                    tile(t, splits[(one, other)[(t - t0) % 2]][0])

            pe.wait_ge(sem("ld_table"), 16)
            for j in range(KT):
                sum_squares("mix", j)
            spread(banks[4])
            stage("qk", "n_mix")
            stage("v", "n_mix")
            all_evacuated(pe, "v")

            def scores(it):
                hh, c = it // TC, it % TC
                if it >= 1:
                    pe.wait_ge(sem("att_scored"), it)
                else:
                    pe.wait_ge(sem("low_done"), splits["n_mix"][1])
                for g in range(3):
                    head = 4 * g + hh
                    tl, b = head // 2, 64 * (head % 2)
                    k0 = max(0, c - 1) * P if g == 0 else 0
                    mm = nc.tensor.matmul(banks[4 + g][:, 0:(c + 1) * P - k0], QK[b:b + 64, tl, c * P:(c + 1) * P],
                                          QK[b:b + 64, 6 + tl, k0:(c + 1) * P], start=True, stop=True)
                mm.then_inc(sem("att_raw"), 1)

            def att_blocks(it):
                c = it % TC
                return [(g, kc) for g in range(3) for kc in range(max(0, c - 1) if g == 0 else 0, c + 1)]

            def turn(it):
                pe.wait_ge(sem("att_p"), it + 1)
                if it >= 1:
                    pe.wait_ge(sem("att_turned"), it)
                for n, _ in enumerate(att_blocks(it)):
                    mm = nc.tensor.transpose(banks[n // 4][:, (n % 4) * P:(n % 4 + 1) * P],
                                             SC[:, it % 2, n * P:(n + 1) * P], ident)
                mm.then_inc(sem("att_t"), 1)

            def weigh(it):
                hh, c = it // TC, it % TC
                pe.wait_ge(sem("att_turned"), it + 1)
                if it == 2 * TC:
                    pe.wait_ge(sem("tmp_ready"), splits["y_attn"][0] + 1)
                b = 64 * (hh % 2)
                bl = att_blocks(it)
                for n, (g, kc) in enumerate(bl):
                    head = 4 * g + hh
                    mm = nc.tensor.matmul(banks[7][b:b + 64, c * P:(c + 1) * P], VT[:, kc, 64 * head:64 * head + 64],
                                          PT[:, n * P:(n + 1) * P], start=(n == 0), stop=(n == len(bl) - 1))
                mm.then_inc(sem("att_y"), 1)

            for it in range(4 * TC + 1):
                if it < 4 * TC:
                    scores(it)
                if it >= 1:
                    turn(it - 1)
                    weigh(it - 1)

            stage("lora", "n_mix")
            pe.wait_ge(sem("lora_ready"), 3)

            def start_group(name, p):
                n = p * len(STEPS) + INDEX[name] - 3
                if n >= 0:
                    emptied(pe, STEPS[n % len(STEPS)][0], n // len(STEPS))
                return rbank(name, p)

            def expanded(name, p, h, lhs, rhs, w=P):
                b = start_group(name, p)
                for i in range(4):
                    c = 4 * h + i
                    mm = nc.tensor.matmul(b[:, w * i:w * (i + 1)], lhs[:, c, :], rhs(c), start=True, stop=True)
                mm.then_inc(sem("rw_made"), 1)

            def turned(name, p, h, src):
                b = start_group(name, p)
                for i in range(4):
                    mm = nc.tensor.transpose(b[:, P * i:P * (i + 1)], src[:, 4 * h + i, :], ident)
                mm.then_inc(sem("rw_made"), 1)

            def side(name, p):
                if (name, p) not in SIDE_AT:
                    return
                b = banks[4]
                side_free(pe, name, p)
                head_of_row = heads[:, 0:P:CH]
                if name == "zw":
                    pe.wait_ge(sem("lw_landed"), 16 * (p + 1))
                    mm = nc.tensor.matmul(b[:], LW_DA[0:64, :], LORA[0:64, :], start=True, stop=True)
                elif name == "za":
                    mm = nc.tensor.matmul(b[:], LW_DA[64:128, :], LORA[64:128, :], start=True, stop=True)
                elif name == "zg":
                    pe.wait_ge(sem("lw_g_landed"), 16 * (p + 1))
                    nc.tensor.matmul(b[:], LW_G[:, 0, :], GD[:, 0, :], start=True, stop=False)
                    mm = nc.tensor.matmul(b[:], LW_G[:, 1, :], GD[:, 1, :], start=False, stop=True)
                elif name in ("ks", "vs"):
                    pe.wait_ge(sem("rw_kk_sq" if name == "ks" else "rw_ysq"), p + 1)
                    src = RK if name == "ks" else YSQ
                    for c in range(TC):
                        mm = nc.tensor.matmul(b[:, 2 * c:2 * c + 2], src[:, c * P:(c + 1) * P], head_of_row, start=True,
                                              stop=True)
                elif name in ("kb", "vb"):
                    spread(b, per=2)
                    return
                elif name == "bo":
                    pe.wait_ge(sem("rw_rk"), p + 1)
                    mm = nc.tensor.matmul(b[:], heads, RK, start=True, stop=True)
                else:
                    emptied(pe, "Y", p)
                    mm = nc.tensor.matmul(b[:], heads, YK, start=True, stop=True)
                mm.then_inc(sem("side_made"), 1)

            t0 = stages["rkv0"][0]
            n_mix = splits["n_mix"][0]
            for t in range(t0, t0 + 4):
                tile(t, n_mix)
            side("zw", 0)
            side("za", 0)
            tile(t0 + 4, n_mix)
            side("ks", 0)
            side("kb", 0)
            tile(t0 + 5, n_mix)
            side("bo", 0)
            for p in range(PAIRS):
                piece = [0]

                def pieces(n):
                    for _ in range(n):
                        if piece[0] < KT * len(beside(p)):
                            tile(beside(p)[piece[0] // KT], n_mix, only=piece[0] % KT)
                            piece[0] += 1

                AR, BX, KX, VX, AX = (a[p % 2] for a in (ARs, BXs, KXs, VXs, AXs))
                pe.wait_ge(sem("rw_ar"), p + 1)
                for h in range(2):
                    expanded(f"bM{h}", p, h, BX, lambda c: AR[:, c, :, :])
                expanded("kM0", p, 0, KX, lambda c: AR[:, c, :, :])
                side("mn", p - 1)
                expanded("kM1", p, 1, KX, lambda c: AR[:, c, :, :])
                pieces(2)
                for h in range(2):
                    pe.wait_ge(sem("rw_tt0"), 2 * p + h + 1)
                    turned(f"tT{h}", p, h, TTX)
                    pieces(2)
                    if h == 0:
                        pe.wait_ge(sem("rw_ax"), p + 1)
                    turned(f"tA{h}", p, h, AX)
                    pieces(1)
                for l in range(1, 6):
                    for h in range(2):
                        if l == 1:
                            emptied(pe, f"tT{h}", p)
                            emptied(pe, f"tA{h}", p)
                        else:
                            emptied(pe, f"D{l - 1}{h}", p)
                        expanded(f"P{l}{h}", p, h, LAB, lambda c: TX[:, c, :])
                    if l == 1:
                        turned("tB0", p, 0, BX)
                        turned("tV0", p, 0, VX)
                    if p + 1 < PAIRS:
                        side({1: "zw", 2: "za", 3: "ks", 4: "kb", 5: "bo"}[l], p + 1)
                    else:
                        pieces(2)
                    for h in range(2):
                        emptied(pe, f"P{l}{h}", p)
                        if l > 1:
                            emptied(pe, f"X{l - 1}{h}", p)
                        expanded(f"D{l}{h}", p, h, TTX, lambda c: AX[:, c, :])
                    if l == 1:
                        turned("tB1", p, 1, BX)
                        turned("tV1", p, 1, VX)
                    if l <= 3:
                        side({1: "vs", 2: "vb", 3: "zg"}[l], p - 1)
                    else:
                        pieces(1)
                    for h in range(2):
                        emptied(pe, f"D{l}{h}", p)
                        turned(f"X{l}{h}", p, h, TX)
                    if l == 1:
                        for h in range(2):
                            turned(f"tK{h}", p, h, KX)
                        for h in range(2):
                            emptied(pe, f"tV{h}", p)
                            expanded(f"Z{h}", p, h, LAK, lambda c: VC[:, c, :], CH)
                for h in range(2):
                    emptied(pe, f"X5{h}", p)
                    emptied(pe, f"Z{h}", p)
                    expanded(f"TAX{h}", p, h, TTX, lambda c: AZ[:, c, :, :])
                pieces(2)
                for h in range(2):
                    emptied(pe, f"TAX{h}", p)
                    emptied(pe, f"tB{h}", p)
                    expanded(f"RM{h}", p, h, AX, lambda c: RM[:, c, :, :])
                    pieces(1)
                for h in range(2):
                    emptied(pe, f"tK{h}", p)
                    b = start_group(f"N{h}", p)
                    for i in range(4):
                        c = 4 * h + i
                        nc.tensor.matmul(b[:, CH * i:CH * (i + 1)], BX[:, c, :], X0C[:, c, :], start=True, stop=False)
                        mm = nc.tensor.matmul(b[:, CH * i:CH * (i + 1)], KX[:, c, :], VC[:, c, :], start=False,
                                              stop=True)
                    mm.then_inc(sem("rw_made"), 1)
                pieces(2)
                b = start_group("scan", p)
                emptied(pe, "N1", p)
                for c in range(1, NC - 1):
                    pe.wait_ge(sem("rw_state"), p * (NC - 2) + c)
                    mm = nc.tensor.matmul(b[:, CH * c:CH * (c + 1)], MCX[:, c, :], SC_[:, c, :], start=True, stop=True)
                    mm.then_inc(sem("rw_made" if c == NC - 2 else "rw_stepped"), 1)
                    pieces(1)
                pieces(2)
                b = start_group("Y", p)
                pe.wait_ge(sem("rw_sx"), p + 1)
                for c in range(NC):
                    o = b[:, CH * c:CH * (c + 1)]
                    nc.tensor.matmul(o, X0X[:, c, :], RM[:, c, 0, :], start=True, stop=False)
                    mm = nc.tensor.matmul(o, VX[:, c, :], MRK[:, c, :], start=False, stop=(c == 0))
                    if c:
                        mm = nc.tensor.matmul(o, SX[:, c, :], AR[:, c, 1, :], start=False, stop=True)
                mm.then_inc(sem("rw_made"), 1)
                pieces(4 * KT)
            t0, t1 = stages["attn_out"]
            side("mn", PAIRS - 1)
            tile(t0, splits["y_attn"][0])
            tile(t0 + 1, splits["y_attn"][0])
            side("vs", PAIRS - 1)
            tile(t0 + 2, splits["y_attn"][0])
            tile(t0 + 3, splits["y_attn"][0])
            side("vb", PAIRS - 1)
            side("zg", PAIRS - 1)

            for t in range(t0 + 4, t1):
                tile(t, splits["y_attn"][0])
            pair_stage("rwkv_out", "n_mix", "y_rwkv")
            for i, t in enumerate(range(*stages["mix_out"])):
                tile(t, splits["merged"][0])
                for j in (range(2 * i, 2 * i + 2) if i < 4 else ()):
                    sum_squares("mem", j, M)
                if i == 4:
                    spread(banks[4], M)
            for j, t in enumerate(range(*stages["mem_k"])):
                tile(t, splits["n_mem"][0], M)
                sum_squares("x", j)
            spread(banks[4])
            stage("mem_v", "n_mem")

            def x_queries(hd):
                for d in range(2):
                    tile(stages["x_q"][0] + 2 * hd + d, splits["n_x"][0])

            x_queries(0)
            for hd in range(XH):
                evacuated(pe, stages["x_q"][0] + 2 * hd + 1)
                if hd == 0:
                    all_evacuated(pe, "mem_v")
                else:
                    pe.wait_ge(sem("x_scored"), hd)
                for c in range(TC):
                    for k in range(2):
                        mm = nc.tensor.matmul(banks[4 + c // 2][:, M * (c % 2):M * (c % 2 + 1)],
                                              XQ[:, 2 * hd + k, c * P:(c + 1) * P], KM[:, 2 * hd + k, :],
                                              start=(k == 0), stop=(k == 1))
                mm.then_inc(sem("x_raw"), 1)
                if hd + 1 < XH:
                    x_queries(hd + 1)
                    t = stages["x_q"][0] + 2 * hd + 4
                    for before in range(t - BANKS, t):
                        evacuated(pe, before)
                pe.wait_ge(sem("x_p"), hd + 1)
                for m in range(2):
                    for c in range(TC):
                        mm = nc.tensor.transpose(banks[m][:, c * P:(c + 1) * P], XP[:, c, m * P:(m + 1) * P], ident)
                mm.then_inc(sem("x_t"), 1)
                pe.wait_ge(sem("x_turned"), hd + 1)
                if hd:
                    pe.wait_ge(sem("tmp_ready"), splits["x_o"][0] + 2 * hd)
                for d in range(2):
                    for m in range(2):
                        mm = nc.tensor.matmul(banks[6 + d][:], VM[:, m, 256 * hd + P * d:256 * hd + P * (d + 1)],
                                              XPT[:, m, :], start=(m == 0), stop=(m == 1))
                mm.then_inc(sem("x_y"), 1)
            stage("x_out", "x_o", norm="ffn")

            def modulation(b):
                pe.wait_ge(sem("ada_used"), KT * (b + 1))
                for i in range(KT * b, KT * (b + 1)):
                    k = i % ADA
                    mm = nc.tensor.matmul(banks[6][:, i:i + 1], ADA_SUM[:, k * P:(k + 1) * P], ones[:, 0:1],
                                          start=True, stop=True)
                mm.then_inc(sem("ada_summed"), 1)

            for c, _ in enumerate(chunks_of(FF1)):
                for name, split in ((f"up{c}", "n_ffn"), (f"down{c}", f"hidden{c}")):
                    for t in range(*stages[name]):
                        tile(t, splits[split][0])
                        i = t - stages["up0"][0] - 2
                        for u in (ada_units(i) if 0 <= i < ADA_SPAN else ()):
                            if u % KT == KT - 1:
                                modulation(u // KT)
                        if name == "down3" and t > stages[name][0]:
                            sum_squares("final", t - stages[name][0] - 1)
            sum_squares("final", KT - 1)
            spread(banks[4])

            for l in range(LAYERS):
                if l == 0:
                    for j in range(KT):
                        sum_squares("n1_0", j)
                    spread(banks[4])
                t0 = stages[f"fourier_in{l}"][0]
                pe.wait_ge(sem("fourier_tables"), 48 * (l + 1))

                def fourier_group(j):
                    g = KT * l + j
                    evacuated(pe, t0 + j)
                    if g >= 1:
                        pe.wait_ge(sem("f_half"), 2 * g)
                    for c in range(TC):
                        mm = nc.tensor.matmul(banks[4 + c // 2][:, 256 * (c % 2):256 * (c % 2 + 1)],
                                              UF[:, j % 2, c * P:(c + 1) * P], CS_FEAT, start=True, stop=True)
                    mm.then_inc(sem("f_feat"), 1)

                def fourier_tokens(j):
                    g = KT * l + j
                    pe.wait_ge(sem("f_half"), 2 * g + 2)
                    if j >= 2:
                        pe.wait_ge(sem("tmp_ready"), splits[f"fourier{l}"][0] + j - 1)
                    elif l:
                        pass
                    for c in range(TC):
                        nc.tensor.matmul(banks[6 + j % 2][:], PF[:, j % 2, c, 0:P], CS_SEQ[:, c, :], start=(c == 0),
                                         stop=False)
                        mm = nc.tensor.matmul(banks[6 + j % 2][:], PF[:, j % 2, c, P:2 * P], SN_SEQ[:, c, :],
                                              start=False, stop=(c == TC - 1))
                    mm.then_inc(sem("f_made"), 1)

                for j in range(KT):
                    tile(t0 + j, splits[f"n1_{l}"][0])
                    if j >= 1:
                        fourier_group(j - 1)
                    if j >= 2:
                        fourier_tokens(j - 2)
                fourier_group(KT - 1)
                fourier_tokens(KT - 2)
                fourier_tokens(KT - 1)
                pair_stage(f"fourier_out{l}", f"n1_{l}", f"fourier{l}")
                def head_tiles(hd, what):
                    for t in range(*stages[f"ret_{what}{l}_{hd}"]):
                        tile(t, splits[f"n1_{l}"][0])

                head_tiles(0, "q")
                head_tiles(0, "k")
                head_tiles(0, "v")
                for hd in range(XH):
                    n = XH * l + hd
                    head_tiles(hd, "g")
                    pe.wait_ge(sem("rotated"), 2 * n + 2)
                    for c in range(TC):
                        if TC * n + c >= 2:
                            pe.wait_ge(sem("ret_masked"), TC * n + c - 1)
                        for k in range(2):
                            mm = nc.tensor.matmul(banks[4 + c % 2][:], RKY[:, k, c * P:(c + 1) * P],
                                                  RQ[:, k, :], start=(k == 0), stop=(k == 1))
                        mm.then_inc(sem("ret_raw"), 1)
                    if hd + 1 < XH:
                        head_tiles(hd + 1, "q")
                    all_evacuated(pe, f"ret_v{l}_{hd}")
                    pe.wait_ge(sem("ret_masked"), TC * (n + 1))
                    if n:
                        pe.wait_ge(sem("ret_scaled"), n)
                    for d in range(2):
                        for c in range(TC):
                            mm = nc.tensor.matmul(banks[6 + d][:], RV[:, c, P * d:P * (d + 1)], RP[:, c, :],
                                                  start=(c == 0), stop=(c == TC - 1))
                        mm.then_inc(sem("ret_y"), 1)
                    if hd + 1 < XH:
                        tile(stages[f"ret_k{l}_{hd + 1}"][0], splits[f"n1_{l}"][0])
                    pe.wait_ge(sem("ret_copied"), 2 * n + 2)
                    for d in range(2):
                        mm = nc.tensor.matmul(banks[6][:], ones, RY[:, d, :], start=(d == 0), stop=(d == 1))
                    mm.then_inc(sem("ret_mean"), 1)
                    if hd + 1 < XH:
                        tile(stages[f"ret_k{l}_{hd + 1}"][0] + 1, splits[f"n1_{l}"][0])
                    pe.wait_ge(sem("ret_sq"), 2 * n + 2)
                    for d in range(2):
                        for c in range(TC):
                            mm = nc.tensor.matmul(banks[7][:, c:c + 1], ROT[:, 2 + d, c * P:(c + 1) * P], ones[:, 0:1],
                                                  start=(d == 0 and c == 0), stop=(d == 1), skip_group_check=True)
                    mm.then_inc(sem("ret_var"), 1)
                    if hd + 1 < XH:
                        head_tiles(hd + 1, "v")
                    else:
                        tile(stages[f"ret_out{l}"][0], splits[f"n1_{l}"][0])
                    spread(banks[6])
                pair_stage(f"ret_out{l}", f"n1_{l}", f"ret{l}", 1)
                stage(f"out{l}", f"m{l}", norm=f"n2_{l}")
                for c, _ in enumerate(chunks_of(FF2)):
                    stage(f"ff_in{l}_{c}", f"n2_{l}")
                    last = c == len(chunks_of(FF2)) - 1
                    after = "out" if l == LAYERS - 1 else f"n1_{l + 1}"
                    stage(f"ff_out{l}_{c}", f"ff{l}_{c}", norm=after if last else None)

        @block.scalar
        def _(act):
            ahead = [0]
            counts = {}

            def done(ins, signal, wait=False):
                counts[signal] = counts.get(signal, 0) + 1
                ins.then_inc(sem(signal), 1)
                if wait:
                    act.wait_ge(sem(signal), counts[signal])

            def follow(t):
                last = min(max(u for u, _, _ in tiles[t]["blocks"]) + 2, n_units - 1)
                if t == len(tiles) - 1:
                    last = n_units - 1
                while ahead[0] <= last:
                    u, k = ahead[0], ahead[0] % RING
                    act.wait_ge(sem(f"w_landed{k}"), 16 * (u // RING + 1))
                    if u >= RING:
                        act.wait_ge(sem("tile_done"), last_tile[u - RING] + 1)
                    nc.scalar.copy(w_hi[:, k, :], w_raw[:, k, :]).then_inc(sem("w_high"), 1)
                    ahead[0] += 1

            def take_tile(t, dst, n=S, func=ACT.Copy, scale=1.0, b0=0):
                follow(t)
                tile_done(act, t)
                nc.scalar.activation(dst, banks[t % BANKS][:, 0:n], func, scale=scale).then_inc(
                    sem(f"bank_free{t % BANKS}"), 1)

            def follow_stage(name, split=None):
                t0, t1 = stages[name]
                q = splits[split][0] if split else None
                for t in range(t0, t1):
                    follow(t)
                    if split:
                        high(q + t - t0)

            def high(q):
                buf, j, free_after = conv[q]
                act.wait_ge(sem("tmp_ready"), q + 1)
                if free_after:
                    tile_done(act, free_after - 1)
                n = M if splits["n_mem"][0] <= q < splits["n_mem"][1] else S
                nc.scalar.copy(acts[buf][:, 0, j, 0:n], tmp[:, q % 2, 0:n]).then_inc(sem("high_done"), 1)

            def highs(split):
                for q in range(*splits[split]):
                    high(q)

            def square(name, j, src, n=S):
                s = squares_before(name) + j
                if s >= 2:
                    act.wait_ge(sem("sq_used"), s - 1)
                nc.scalar.activation(squares[:, s % 2, 0:n], src, ACT.Square).then_inc(sem("sq_ready"), 1)

            act.dma_start(table[:], ap["table"]).then_inc(sem("ld_table"), 16)
            act.dma_start(H, ap["x"]).then_inc(sem("ld_x"), 16)
            act.dma_start(params[:], ap["params"]).then_inc(sem("ld_params"), 16)
            act.dma_start(DIST, ap["dist"]).then_inc(sem("ld_dist"), 16)
            act.wait_ge(sem("ld_x"), 16)
            for j in range(KT):
                square("mix", j, H[:, j, :])
            follow(0)
            highs("n_mix")
            for t in range(*stages["qk"]):
                j = t - stages["qk"][0]
                take_tile(t, QK[:, j, :], scale=0.125 if j < 6 else 1.0)
            for t in range(*stages["v"]):
                T = tiles[t]
                take_tile(t, VT[:, T["token"], T["col"]:T["col"] + T["width"]], T["width"])
            q_attn = splits["y_attn"][0]

            def turned_out(it):
                act.wait_ge(sem("att_t"), it + 1)
                if it:
                    act.wait_ge(sem("att_y"), it)
                c = it % TC
                nb = (c + 1) * 2 + min(c + 1, 2)
                for i in range((nb + 3) // 4):
                    w = min(4, nb - 4 * i) * P
                    ins = nc.scalar.copy(PT[:, 512 * i:512 * i + w], banks[i][:, 0:w])
                done(ins, "att_turned")

            for it in range(4 * TC):
                c = it % TC
                if it >= 1:
                    turned_out(it - 1)
                act.wait_ge(sem("att_max"), it + 1)
                nb = (c + 1) * 2 + min(c + 1, 2)
                done(nc.scalar.activation(SC[:, it % 2, 0:nb * P], SC[:, it % 2, 0:nb * P], ACT.Exp,
                                          bias=att_stat[:, it % 2, 0:1], scale=1.0,
                                          accum_out=att_stat[:, it % 2, 1:2]), "att_exp")
                if it == 2 * TC + 2:
                    high(q_attn)
            turned_out(4 * TC - 1)
            high(q_attn + 1)

            def to_raw(t, i):
                if i >= 2:
                    act.wait_ge(sem("shift_done"), i - 1)
                take_tile(t, RAW[:, i % 2, 8:8 + S])

            act.wait_ge(sem("rw_zeroed"), 1)
            act.dma_start(LW_DA, ap["lora_w"][0, :, 0, :]).then_inc(sem("lw_landed"), 16)
            act.dma_start(LW_G, ap["lora_w"][0, :, 1:3, :]).then_inc(sem("lw_g_landed"), 16)
            for i in range(3):
                to_raw(stages["lora"][0] + i, i)
                act.wait_ge(sem("shift_done"), i + 1)
                if i == 0:
                    done(nc.scalar.activation(LORA[0:64, :], LORA[0:64, :], ACT.Tanh), "lora_ready")
                else:
                    done(nc.scalar.activation(GD[:, i - 1, :], GD[:, i - 1, :], ACT.Sigmoid), "lora_ready")

            def raw(p, i):
                to_raw(stages[f"rkv{p}"][0] + i, 3 + 3 * p + i)

            def half_tanh(name, p, dst, bias):
                side_made(act, name, p)
                nc.scalar.activation(dst, banks[4][:], ACT.Tanh, bias=half_bias[:, bias + p:bias + p + 1],
                                     scale=0.5).then_inc(sem("side_emptied"), 1)

            def key_squares(p):
                act.wait_ge(sem("rw_kk"), p + 1)
                done(nc.scalar.activation(RK, KK, ACT.Square), "rw_kk_sq")

            def decays(p):
                act.wait_ge(sem("rw_cs"), p + 1)
                nc.scalar.activation(W, CS, ACT.Exp, scale=LOG_DECAY)
                nc.scalar.activation(WI, CS, ACT.Exp, scale=-LOG_DECAY)
                done(nc.scalar.activation(WX, WX, ACT.Exp, scale=LOG_DECAY), "rw_w")

            def spread_values(p):
                for h in range(2):
                    r = slice(64 * h, 64 * h + 64)
                    nc.scalar.copy(VXs[p % 2][r, :, 64 * h:64 * h + 64], V[r, :].rearrange("p (c t) -> p c t", t=CH))

            def spread_a(p):
                act.wait_ge(sem("rw_a"), p + 1)
                for h in range(2):
                    r = slice(64 * h, 64 * h + 64)
                    ins = nc.scalar.copy(AXs[p % 2][r, :, 64 * h:64 * h + 64], ARs[p % 2][r, :, 0, :])
                done(ins, "rw_ax")

            for i in range(3):
                raw(0, i)
            half_tanh("zw", 0, SW, 0)
            half_tanh("za", 0, A_, 8)
            key_squares(0)
            decays(0)
            spread_values(0)
            spread_a(0)
            follow(stages["rkv1"][0])
            follow(stages["rkv1"][0] + 1)
            follow(stages["rkv1"][0] + 2)
            for p in range(PAIRS):
                BX, KX, VX = BXs[p % 2], KXs[p % 2], VXs[p % 2]
                more = p + 1 < PAIRS
                if not more:
                    for j, t in enumerate(beside(p - 1)):
                        take_tile(t, GATES[:, j, :])
                if more:
                    side_made(act, "za", p)
                    act.dma_start(LW_DA, ap["lora_w"][p + 1, :, 0, :]).then_inc(sem("lw_landed"), 16)

                def halves(name, h, wide, compact):
                    made(act, name, p)
                    src = rbank(name, p)[:].rearrange("p (c s) -> p c s", s=P)
                    cs = slice(4 * h, 4 * h + 4)
                    if wide is not None:
                        ins = nc.scalar.activation(wide[:, cs, :], src, ACT.Copy)
                    if compact is not None:
                        for i in range(2):
                            r = slice(64 * i, 64 * i + 64)
                            ins = nc.scalar.activation(compact[r, cs, :], src[r, :, 64 * i:64 * i + 64], ACT.Copy)
                    ins.then_inc(sem("rw_emptied_a"), 1)

                for h in range(2):
                    halves(f"tT{h}", h, TX, None)
                    halves(f"tA{h}", h, None, AZ[:, :, 0, :])
                if p:
                    act.wait_ge(sem("rw_yc"), p)
                    done(nc.scalar.activation(YSQ, YC, ACT.Square), "rw_ysq")
                for h in range(2):
                    halves(f"tB{h}", h, BX, RM[:, :, 1, :])
                    halves(f"tV{h}", h, VX, VC)
                    if more and h == 0:
                        half_tanh("zw", p + 1, SW, 0)
                    if more:
                        raw(p + 1, h)
                nxt = beside(p)
                for l in range(1, 6):
                    if nxt and l in (1, 2, 4):
                        follow(nxt.pop(0))
                    if more and l == 2:
                        half_tanh("za", p + 1, A_, 8)
                        key_squares(p + 1)
                    for h in range(2):
                        halves(f"X{l}{h}", h, TTX, None)
                    if l == 1:
                        if more:
                            raw(p + 1, 2)
                        for h in range(2):
                            halves(f"tK{h}", h, KX, None)
                        for h in range(2):
                            made(act, f"Z{h}", p)
                            nc.scalar.activation(AZ[:, 4 * h:4 * h + 4, 1, :],
                                                 rbank(f"Z{h}", p)[:, 0:256].rearrange("p (c s) -> p c s", s=CH),
                                                 ACT.Copy).then_inc(sem("rw_emptied_a"), 1)
                    if more and l == 3:
                        decays(p + 1)
                        spread_values(p + 1)
                    if p and l == 4:
                        act.wait_ge(sem("y_out"), p)
                        act.dma_start(y_scratch[p - 1], YO[:, (p - 1) % 2, :]).then_inc(sem(f"y_stored{(p - 1) % 2}"), 16)
                        act.dma_start(LW_G, ap["lora_w"][p, :, 1:3, :]).then_inc(sem("lw_g_landed"), 16)
                if more:
                    spread_a(p + 1)
                while nxt:
                    follow(nxt.pop(0))
                made(act, "Y", p)
                nc.scalar.activation(YK, rbank("Y", p)[:], ACT.Copy).then_inc(sem("rw_emptied_a"), 1)
            for j, t in enumerate(beside(PAIRS - 1)):
                take_tile(t, GATES[:, 4 + j, :])
            act.wait_ge(sem("y_stored0"), 16 * PAIRS // 2)
            act.wait_ge(sem("y_stored1"), 16 * (PAIRS // 2 - 1))
            act.dma_start(YB[:, 0:PAIRS - 1, :], y_scratch.rearrange("j p t -> p j t")).then_inc(sem("ld_y"), 16)
            act.dma_start(MEM, ap["mem"]).then_inc(sem("ld_mem"), 16)
            act.wait_ge(sem("rw_yc"), PAIRS)
            done(nc.scalar.activation(YSQ, YC, ACT.Square), "rw_ysq")
            for t in range(*stages["attn_out"]):
                follow(t)
                if t == stages["attn_out"][0] + 3:
                    break
            q = splits["y_rwkv"][0]
            for j in range(3):
                high(q + j)
            for j in range(KT):
                done(nc.scalar.activation(GATES[:, j, :], GATES[:, j, :], ACT.Sigmoid), "gate_a_ready")
            for j in range(3, KT):
                high(q + j)
            act.dma_start(H, ap["x"]).then_inc(sem("ld_x"), 16)
            for t in range(stages["attn_out"][0] + 4, stages["attn_out"][1]):
                follow(t)

            def gates(name, t_gates, each=1):
                for t in t_gates:
                    i = counts.get("gate_ready", 0)
                    if i >= 2:
                        act.wait_ge(sem("gate_used"), i - 1)
                    follow(t)
                    tile_done(act, t)
                    nc.scalar.activation(gate_buf[:, i % 2, :], banks[t % BANKS][:], ACT.Sigmoid).then_inc(
                        sem(f"bank_free{t % BANKS}"), 1)
                    counts["gate_ready"] = i + 1
                    if each == 2:
                        follow(t + 1)

            gates("rwkv_out", range(stages["rwkv_out"][0], stages["rwkv_out"][1], 2), 2)
            highs("merged")
            act.wait_ge(sem("ld_mem"), 16)
            q = splits["n_mem"][0]
            for i, t in enumerate(range(*stages["mix_out"])):
                follow(t)
                for j in range(2 * (i % 4), 2 * (i % 4) + 2):
                    if i < 4:
                        square("mem", j, MEM[:, j, :], M)
                    else:
                        high(q + j)
            for j, t in enumerate(range(*stages["mem_k"])):
                evacuated(act, stages["mix_out"][0] + j)
                square("x", j, H[:, j, :])
                take_tile(t, KM[:, j, :], M)
            q = splits["n_x"][0]
            for i, t in enumerate(range(*stages["mem_v"])):
                T = tiles[t]
                follow(t)
                high(q + 2 * i)
                high(q + 2 * i + 1)
                take_tile(t, VM[:, T["token"], T["col"]:T["col"] + T["width"]], T["width"])

            def x_queries(hd):
                for j in range(2 * hd, 2 * hd + 2):
                    take_tile(stages["x_q"][0] + j, XQ[:, j, :], scale=1.0 / 16)

            x_queries(0)
            for hd in range(XH):
                act.wait_ge(sem("x_max"), hd + 1)
                for c in range(TC):
                    ins = nc.scalar.activation(XP[:, c, :], banks[4 + c // 2][:, M * (c % 2):M * (c % 2 + 1)], ACT.Exp,
                                               bias=x_stat[:, c, 0:1], scale=1.0, accum_out=x_stat[:, c, 1:2])
                done(ins, "x_scored")
                if hd + 1 < XH:
                    x_queries(hd + 1)
                act.wait_ge(sem("x_t"), hd + 1)
                if hd:
                    act.wait_ge(sem("x_y"), hd)
                for m in range(2):
                    ins = nc.scalar.copy(XPT[:, m, :], banks[m][:])
                done(ins, "x_turned")
                for d in range(2):
                    high(splits["x_o"][0] + 2 * hd + d)
            t0 = stages["x_out"][0]
            act.wait_ge(sem("ld_params"), 16)
            done(nc.scalar.activation(c_act, prm("c", 0, 8), ACT.Silu), "c_ready")
            for t in range(*stages["x_out"]):
                follow(t)
                evacuated(act, t)
                square("ffn", t - t0, H[:, t - t0, :])
            highs("n_ffn")
            for c, _ in enumerate(chunks_of(FF1)):
                q = splits[f"hidden{c}"][0]
                t0, t1 = stages[f"up{c}"]
                for t in range(t0, t1):
                    i = 8 * c + t - t0
                    follow(t)
                    tile_done(act, t)
                    if t - t0 >= 2:
                        act.wait_ge(sem("tmp_ready"), q + t - t0 - 1)
                    nc.scalar.activation(RELU[:, i % 2, :], banks[t % BANKS][:], ACT.Relu).then_inc(
                        sem(f"bank_free{t % BANKS}"), 1)
                    if t > t0:
                        high(q + t - t0 - 1)
                high(q + t1 - t0 - 1)
                t0, t1 = stages[f"down{c}"]
                for t in range(t0, t1):
                    follow(t)
                    if c == 3:
                        evacuated(act, t)
                        square("final", t - t0, H[:, t - t0, :])

            for l in range(LAYERS):
                for j in (range(KT) if l == 0 else ()):
                    act.wait_ge(sem("final_done"), j + 1)
                    square("n1_0", j, H[:, j, :])
                act.dma_start(CS_SEQ, ap["dft_cos"]).then_inc(sem("fourier_tables"), 16)
                act.dma_start(SN_SEQ, ap["dft_sin"]).then_inc(sem("fourier_tables"), 16)
                act.dma_start(CS_FEAT, ap["dft_feature"]).then_inc(sem("fourier_tables"), 16)
                highs(f"n1_{l}")
                t0 = stages[f"fourier_in{l}"][0]
                for j in range(KT + 2):
                    if j < KT:
                        if KT * l + j >= 2:
                            act.wait_ge(sem("f_feat"), KT * l + j - 1)
                        take_tile(t0 + j, UF[:, j % 2, :])
                    if 1 <= j <= KT:
                        g = KT * l + j - 1
                        act.wait_ge(sem("f_feat"), g + 1)
                        if g >= 2:
                            act.wait_ge(sem("f_made"), g - 1)
                        for i in range(2):
                            done(nc.scalar.copy(PF[:, (j - 1) % 2, 2 * i:2 * i + 2, :],
                                                banks[4 + i][:].rearrange("p (c f) -> p c f", f=256)), "f_half")
                    if j >= 2:
                        high(splits[f"fourier{l}"][0] + j - 2)
                gates("", range(stages[f"fourier_out{l}"][0], stages[f"fourier_out{l}"][1], 2), 2)

                def take_values(hd):
                    if XH * l + hd:
                        act.wait_ge(sem("ret_y"), 2 * (XH * l + hd))
                    t0 = stages[f"ret_v{l}_{hd}"][0]
                    for t in range(t0, t0 + TC):
                        take_tile(t, RV[:, t - t0, :], 256)

                for hd in range(XH):
                    n = XH * l + hd
                    for what in "qk":
                        for t in range(*stages[f"ret_{what}{l}_{hd}"]):
                            follow(t)
                    if hd == 0:
                        act.wait_ge(sem("gate_used"), counts["gate_ready"])
                        act.dma_start(COS, ap["rotary"][:, 0, :]).then_inc(sem("ret_tables"), 16)
                        act.dma_start(SIN, ap["rotary"][:, 1, :]).then_inc(sem("ret_tables"), 16)
                    else:
                        act.wait_ge(sem("ret_masked"), TC * n)
                    act.dma_start(STRIP, ap["strips"][hd]).then_inc(sem("strip_landed"), 16)
                    if hd == 0:
                        take_values(0)
                    for t in range(*stages[f"ret_g{l}_{hd}"]):
                        i = t - stages[f"ret_g{l}_{hd}"][0]
                        if n:
                            act.wait_ge(sem("tmp_ready"), splits[f"ret{l}"][0] + 2 * hd)
                        take_tile(t, RG[:, i, :], func=ACT.Silu)
                    if hd + 1 < XH:
                        for t in range(*stages[f"ret_q{l}_{hd + 1}"]):
                            follow(t)
                    for d in range(2):
                        act.wait_ge(sem("ret_y"), 2 * n + d + 1)
                        done(nc.scalar.copy(RY[:, d, :], banks[6 + d][:]), "ret_copied")
                    if hd + 1 < XH:
                        for t in range(*stages[f"ret_k{l}_{hd + 1}"]):
                            follow(t)
                    for d in range(2):
                        act.wait_ge(sem("ret_centred"), 2 * n + d + 1)
                        done(nc.scalar.activation(ROT[:, 2 + d, :], RY[:, d, :], ACT.Square), "ret_sq")
                    if hd + 1 < XH:
                        take_values(hd + 1)
                    else:
                        follow(stages[f"ret_out{l}"][0])
                    for d in range(2):
                        high(splits[f"ret{l}"][0] + 2 * hd + d)
                gates("", range(stages[f"ret_out{l}"][0], stages[f"ret_out{l}"][1], 2), 2)
                highs(f"m{l}")
                t0 = stages[f"out{l}"][0]
                for t in range(*stages[f"out{l}"]):
                    follow(t)
                    evacuated(act, t)
                    square(f"n2_{l}", t - t0, H[:, t - t0, :])
                highs(f"n2_{l}")
                for c, (a, n) in enumerate(chunks_of(FF2)):
                    t0 = stages[f"ff_in{l}_{c}"][0]
                    q = splits[f"ff{l}_{c}"][0]
                    for j in range(n):
                        i = FF2 * l + a + j
                        for half in range(2):
                            if 2 * i + half >= 2:
                                act.wait_ge(sem("conv_done"), 2 * i + half - 1)
                            take_tile(t0 + 2 * j + half, FRAW[:, half, 8:8 + S])
                        act.wait_ge(sem("conv_done"), 2 * i + 1)
                        done(nc.scalar.activation(CONV[:, i % 2, 0, :], CONV[:, i % 2, 0, :], ACT.Gelu), "gelu")
                        if j:
                            high(q + j - 1)
                    high(q + n - 1)
                    t0 = stages[f"ff_out{l}_{c}"][0]
                    for t in range(t0, t0 + 8):
                        follow(t)
                        if c == len(chunks_of(FF2)) - 1:
                            evacuated(act, t)
                            square("out" if l == LAYERS - 1 else f"n1_{l + 1}", t - t0, H[:, t - t0, :])

        @block.vector
        def _(dve):
            counts = {}
            V_ = nc.vector

            def do(ins, signal="vector_step", value=None):
                if value is None:
                    value = counts[signal] = counts.get(signal, 0) + 1
                ins.then_inc(sem(signal), 1)
                dve.wait_ge(sem(signal), value)

            def take_tile(t, make_op):
                tile_done(dve, t)
                do(make_op(banks[t % BANKS]), f"bank_free{t % BANKS}", t // BANKS + 1)

            def low(q):
                buf, j, _ = conv[q]
                n = M if splits["n_mem"][0] <= q < splits["n_mem"][1] else S
                dve.wait_ge(sem("high_done"), q + 1)
                do(V_.tensor_tensor(acts[buf][:, 1, j, 0:n], tmp[:, q % 2, 0:n],
                                    acts[buf][:, 0, j, 0:n].bitcast(F32), ALU.subtract), "low_done")

            def split_all(split, make_op):
                q0, q1 = splits[split]
                for q in range(q0, q1):
                    make_op(q - q0, tmp[:, q % 2, :])
                    if q > q0:
                        low(q - 1)
                low(q1 - 1)

            def statistic(src, count, cols, eps):
                r = counts.get("stats_ready", 0)
                if r >= 2:
                    dve.wait_ge(sem("spread"), r - 1)
                if eps is None:
                    do(V_.tensor_scalar(rsqrt(r)[:, 0:cols], src, count, None, ALU.max), "stats_ready")
                else:
                    do(V_.tensor_scalar(rsqrt(r)[:, 0:cols], src, 1.0 / count, eps, ALU.mult, ALU.add), "stats_ready")

            def spread_out():
                dve.wait_ge(sem("spread"), counts["stats_ready"])

            def inverse_deviation(name, n=S):
                dve.wait_ge(sem("sq_used"), squares_before(name) + KT)
                statistic(banks[5][:, 0:n // P], D, n // P, EPS)
                spread_out()

            def scaled_by(dst, src, g, signal, n=S):
                do(V_.scalar_tensor_tensor(dst, src, g, banks[4][:, 0:n], ALU.mult, ALU.mult), signal)

            def add_to_h(t, j, scale=None):
                if scale is None:
                    take_tile(t, lambda b: V_.tensor_tensor(H[:, j, :], H[:, j, :], b[:], ALU.add))
                else:
                    take_tile(t, lambda b: V_.scalar_tensor_tensor(H[:, j, :], b[:], scale, H[:, j, :], ALU.mult,
                                                                   ALU.add))

            dve.wait_ge(sem("ld_x"), 16)
            dve.wait_ge(sem("ld_params"), 16)
            inverse_deviation("mix")
            split_all("n_mix", lambda j, d: scaled_by(d, H[:, j, :], prm("g_mix", j), "tmp_ready"))

            for a in (BX1, KX1, VX1, AX1):
                do(V_.memset(a, 0.0))

            dve.wait_ge(sem("ld_dist"), 16)
            q_attn = splits["y_attn"][0]

            def weights(it):
                dve.wait_ge(sem("att_exp"), it + 1)
                w = ((it % TC + 1) * 2 + min(it % TC + 1, 2)) * P
                st = att_stat[:, it % 2, :]
                do(V_.reciprocal(st[:, 2:3], st[:, 1:2]))
                do(V_.tensor_scalar(SC[:, it % 2, 0:w], SC[:, it % 2, 0:w], st[:, 2:3], None, ALU.mult), "att_p")

            for it in range(4 * TC):
                hh, c = it // TC, it % TC
                if it >= 1:
                    weights(it - 1)
                dve.wait_ge(sem("att_raw"), it + 1)
                if it >= 2:
                    dve.wait_ge(sem("att_t"), it - 1)
                at = 0
                for g in range(3):
                    w = (min(c + 1, 2) if g == 0 else c + 1) * P
                    d_end = (256, 768, 1280)[g]
                    do(V_.scalar_tensor_tensor(SC[:, it % 2, at:at + w], DIST[:, d_end - w:d_end],
                                               -float(2.0 ** (-8.0 * (4 * g + hh + 1) / AH)), banks[4 + g][:, 0:w],
                                               ALU.mult, ALU.add), "att_scored" if g == 2 else "vector_step")
                    at += w
                do(V_.tensor_reduce(att_stat[:, it % 2, 0:1], SC[:, it % 2, 0:at], AX_X, ALU.max, negate=True),
                   "att_max")
                if it == 2 * TC + 1:
                    dve.wait_ge(sem("att_y"), 2 * TC)
                    do(V_.tensor_copy(tmp[:, q_attn % 2, :], banks[7][:]), "tmp_ready")
            weights(4 * TC - 1)
            low(q_attn)
            dve.wait_ge(sem("att_y"), 4 * TC)
            do(V_.tensor_copy(tmp[:, (q_attn + 1) % 2, :], banks[7][:]), "tmp_ready")
            low(q_attn + 1)

            for a in (BX0, KX0, VX0, AX0, RAW):
                do(V_.memset(a, 0.0))
            do(V_.tensor_scalar(half_bias, prm("w0", 0, 16), 0.5, None, ALU.mult), "rw_zeroed")

            def shift(t, i, mu, dst):
                evacuated(dve, t)
                raw = RAW[:, i % 2, :]
                do(V_.tensor_tensor(DIFF, raw[:, 7:7 + S], raw[:, 8:8 + S], ALU.subtract))
                do(V_.scalar_tensor_tensor(dst, DIFF, prm("mu", mu), raw[:, 8:8 + S], ALU.mult, ALU.add), "shift_done")

            for i, dst in enumerate((LORA, GD[:, 0, :], GD[:, 1, :])):
                shift(stages["lora"][0] + i, i, 24 + i, dst)

            def by_chunk(a):
                return a.rearrange("p (c t) -> p c t", t=CH)

            def four(a):
                return a[:].rearrange("p (c s) -> p c s", s=P)

            def twice(a):
                return a.unsqueeze(2).to_broadcast([P, 4, 2, CH])

            def both(a):
                return a.rearrange("p c (h s) -> p c h s", h=2)

            def mask2(m):
                return m.rearrange("p (h s) -> p h s", h=2).unsqueeze(1).to_broadcast([P, 4, 2, CH])

            def mask1(m):
                return m.unsqueeze(1).to_broadcast([P, 4, CH])

            def side_emptied(ins, name, p):
                do(ins, "side_emptied", SIDE_AT[name, p] + 1)

            def shifts(p, which):
                for i in which:
                    shift(stages[f"rkv{p}"][0] + i, 3 + 3 * p + i, 8 * i + p, (R, K, V)[i])

            def keys(p):
                do(V_.tensor_scalar(KK, K, prm("k_k", p), None, ALU.mult), "rw_kk")

            def decay_sums(p):
                side_made(dve, "zw", p)
                dve.wait_ge(sem("side_emptied"), SIDE_AT["zw", p] + 1)
                do(V_.tensor_scalar(SW, SW, 0.5, 0.5, ALU.mult, ALU.add))
                do(V_.tensor_tensor_scan(CS, reset, SW, 0.0, ALU.mult, ALU.add))
                do(V_.tensor_tensor(WX, CS, SW, ALU.subtract), "rw_cs")

            def key_statistic(p):
                side_made(dve, "ks", p)
                r = counts.get("stats_ready", 0)
                if r >= 2:
                    dve.wait_ge(sem("spread"), r - 1)
                do(V_.tensor_scalar(rsqrt(r), banks[4][:, 0:8], 1e-24, None, ALU.max), "stats_ready")
                side_emptied(V_.memset(spare, 0.0), "ks", p)

            def rates(p):
                dve.wait_ge(sem("side_emptied"), SIDE_AT["za", p] + 1)
                do(V_.tensor_scalar(A_, A_, 0.5, 0.5, ALU.mult, ALU.add))
                do(V_.tensor_scalar(SW, A_, -1.0, prm("k_a", p), ALU.add, ALU.mult))
                do(V_.scalar_tensor_tensor(K, SW, 1.0, K, ALU.add, ALU.mult))
                do(V_.scalar_tensor_tensor(RK, R, prm("r_k", p), K, ALU.mult, ALU.mult), "rw_rk")

            def unit_keys(p):
                spread_out()
                side_emptied(V_.tensor_tensor(KK, KK, banks[4][:], ALU.mult), "kb", p)
                do(V_.tensor_tensor(A_, A_, KK, ALU.mult))
                dve.wait_ge(sem("rw_w"), p + 1)
                do(V_.scalar_tensor_tensor(ARs[p % 2][:, :, 0, :], by_chunk(KK), -1.0, by_chunk(WX), ALU.mult, ALU.mult),
                   "rw_a")

            def operands(p):
                for h in range(2):
                    r = slice(64 * h, 64 * h + 64)
                    do(V_.tensor_tensor(BXs[p % 2][r, :, r], by_chunk(A_)[r], by_chunk(WI)[r], ALU.mult))
                    do(V_.tensor_tensor(KXs[p % 2][r, :, r], by_chunk(K)[r], by_chunk(WI)[r], ALU.mult))
                do(V_.tensor_copy(w_ends[:, p % 2, :], by_chunk(W)[:, :, CH - 1]))
                do(V_.tensor_tensor(ARs[p % 2][:, :, 1, :], by_chunk(R), by_chunk(W), ALU.mult), "rw_ar")

            def bonus(p):
                side_made(dve, "bo", p)
                side_emptied(V_.tensor_tensor(BOs[p % 2], banks[4][:], V, ALU.mult), "bo", p)

            def centre(p):
                side_made(dve, "mn", p)
                side_emptied(V_.scalar_tensor_tensor(YC, banks[4][:], -1.0 / CH, YK, ALU.mult, ALU.add), "mn", p)
                do(V_.memset(spare, 0.0), "rw_yc")

            def norm_statistic(p):
                side_made(dve, "vs", p)
                statistic(banks[4][:, 0:8], CH, 8, GN_EPS)
                side_emptied(V_.memset(spare, 0.0), "vs", p)

            def normalise(p):
                spread_out()
                side_emptied(V_.tensor_tensor(YC, YC, banks[4][:], ALU.mult), "vb", p)
                do(V_.tensor_scalar(YC, YC, prm("gn_w", p), prm("gn_b", p), ALU.mult, ALU.add))
                do(V_.tensor_tensor(YC, YC, BOs[p % 2], ALU.add))

            def finish(p):
                if p >= 2:
                    dve.wait_ge(sem(f"y_stored{p % 2}"), 16 * (p // 2))
                side_made(dve, "zg", p)
                side_emptied(V_.tensor_tensor(YO[:, p % 2, :], YC, banks[4][:], ALU.mult), "zg", p)
                do(V_.memset(spare, 0.0), "y_out" if p + 1 < PAIRS else "tmp_ready")

            shifts(0, (0, 1, 2))
            keys(0)
            decay_sums(0)
            key_statistic(0)
            rates(0)
            unit_keys(0)
            operands(0)
            bonus(0)
            for p in range(PAIRS):
                AR, AX = ARs[p % 2], AXs[p % 2]
                more = p + 1 < PAIRS
                def masked(name, cs, wide, narrow):
                    src = four(rbank(name, p))
                    made(dve, name, p)
                    do(V_.tensor_tensor(both(wide[:, cs, :]), twice(src[:, :, 0:CH]), mask2(strict), ALU.mult))
                    do(V_.tensor_tensor(narrow[:, cs, :], src[:, :, CH:P], mask1(incl), ALU.mult), "rw_emptied_v")

                for h in range(2):
                    cs = slice(4 * h, 4 * h + 4)
                    masked(f"bM{h}", cs, LAB, RM[:, :, 0, :])
                    do(V_.tensor_tensor(both(TTX[:, cs, :]), both(LAB[:, cs, :]), twice(mask1(level[:, 0, :])), ALU.mult))
                    do(V_.tensor_tensor(TTX[:, cs, :], TTX[:, cs, :], ident.unsqueeze(1).to_broadcast([P, 4, P]),
                                        ALU.add), "rw_tt0")
                masked("kM0", slice(0, 4), LAK, MRK)
                if p:
                    centre(p - 1)
                masked("kM1", slice(4, 8), LAK, MRK)
                for l in range(1, 6):
                    for h in range(2):
                        cs = slice(4 * h, 4 * h + 4)
                        made(dve, f"P{l}{h}", p)
                        do(V_.tensor_tensor(both(AX[:, cs, :]), both(four(rbank(f"P{l}{h}", p))),
                                            twice(mask1(level[:, l, :])), ALU.mult), "rw_emptied_v")
                    if l == 2 and p:
                        norm_statistic(p - 1)
                    if l == 3 and more:
                        decay_sums(p + 1)
                    for h in range(2):
                        cs = slice(4 * h, 4 * h + 4)
                        made(dve, f"D{l}{h}", p)
                        do(V_.tensor_tensor(TX[:, cs, :], TX[:, cs, :], four(rbank(f"D{l}{h}", p)), ALU.add),
                           "rw_emptied_v")
                    if l == 1 and more:
                        shifts(p + 1, (0, 1))
                        keys(p + 1)
                    if l == 2 and p:
                        normalise(p - 1)
                    if l == 2 and more:
                        shifts(p + 1, (2,))
                    if l == 3 and more:
                        key_statistic(p + 1)
                        rates(p + 1)
                    if l == 3 and p:
                        finish(p - 1)
                    if l == 4 and more:
                        unit_keys(p + 1)
                    if l == 5 and more:
                        operands(p + 1)
                for h in range(2):
                    cs = slice(4 * h, 4 * h + 4)
                    made(dve, f"TAX{h}", p)
                    src = four(rbank(f"TAX{h}", p))
                    do(V_.tensor_tensor(both(AX[:, cs, :]), twice(src[:, :, 0:CH]), mask2(heads), ALU.mult))
                    do(V_.tensor_tensor(both(X0X[:, cs, :]), twice(src[:, :, CH:P]), mask2(heads), ALU.mult))
                    do(V_.tensor_copy(X0C[:, cs, :], src[:, :, CH:P]), "rw_emptied_v")
                for h in range(2):
                    cs = slice(4 * h, 4 * h + 4)
                    made(dve, f"RM{h}", p)
                    src = four(rbank(f"RM{h}", p))
                    do(V_.tensor_tensor(AR[:, cs, 1, :], AR[:, cs, 1, :], src[:, :, 0:CH], ALU.add))
                    do(V_.tensor_tensor(both(MCX[:, cs, :]), twice(src[:, :, CH:P]), mask2(heads), ALU.mult))
                    do(V_.tensor_tensor(MCX[:, cs, :], MCX[:, cs, :], ident.unsqueeze(1).to_broadcast([P, 4, P]),
                                        ALU.add), "rw_emptied_v")
                w_end = w_ends[:, p % 2, :]
                for h in range(2):
                    cs = slice(4 * h, 4 * h + 4)
                    made(dve, f"N{h}", p)
                    do(V_.tensor_tensor(NP_[:, cs, :], rbank(f"N{h}", p)[:, 0:256].rearrange("p (c s) -> p c s", s=CH),
                                        w_end[:, cs].unsqueeze(2).to_broadcast([P, 4, CH]), ALU.mult), "rw_emptied_v")
                do(V_.tensor_copy(SC_[:, 1, :], NP_[:, 0, :]), "rw_state")
                for c in range(1, NC - 1):
                    last = c == NC - 2
                    if last:
                        made(dve, "scan", p)
                    else:
                        dve.wait_ge(sem("rw_stepped"), p * (NC - 3) + c)
                    do(V_.scalar_tensor_tensor(SC_[:, c + 1, :], rbank("scan", p)[:, CH * c:CH * (c + 1)],
                                               w_end[:, c:c + 1], NP_[:, c, :], ALU.mult, ALU.add),
                       "rw_emptied_v" if last else "rw_state")
                for h in range(2):
                    cs = slice(4 * h, 4 * h + 4)
                    if h == 0:
                        do(V_.memset(SC_[:, 0, :], 0.0))
                    do(V_.tensor_tensor(both(SX[:, cs, :]), twice(SC_[:, cs, :]), mask2(heads), ALU.mult),
                       "rw_sx" if h else "vector_step")
                if more:
                    bonus(p + 1)
            q = splits["y_rwkv"][0]

            def split_pairs(j0, j1):
                for j in range(j0, j1):
                    do(V_.tensor_copy(tmp[:, (q + j) % 2, :], YB[:, j, :]), "tmp_ready")
                    if j > j0:
                        low(q + j - 1)
                low(q + j1 - 1)

            centre(PAIRS - 1)
            norm_statistic(PAIRS - 1)
            dve.wait_ge(sem("ld_y"), 16)
            split_pairs(0, 3)
            normalise(PAIRS - 1)
            split_pairs(3, PAIRS - 1)
            finish(PAIRS - 1)
            low(q + PAIRS - 1)

            for j, t in enumerate(range(*stages["attn_out"])):
                dve.wait_ge(sem("gate_a_ready"), j + 1)
                take_tile(t, lambda b: V_.tensor_tensor(MERGED[:, j, :], GATES[:, j, :], b[:], ALU.mult))

            def gate():
                i = counts["gates"] = counts.get("gates", -1) + 1
                return gate_buf[:, i % 2, :]

            def gated_pairs(name, first):
                t0, t1 = stages[name]
                for j in range(KT):
                    g = gate()
                    evacuated(dve, t0 + 2 * j)
                    dst = MERGED[:, j, :] if first else g
                    take_tile(t0 + 2 * j + 1, lambda b: V_.tensor_tensor(dst, g, b[:], ALU.mult))
                    if first:
                        do(V_.memset(spare, 0.0), "gate_used")
                    else:
                        do(V_.tensor_tensor(MERGED[:, j, :], MERGED[:, j, :], g, ALU.add), "gate_used")

            gated_pairs("rwkv_out", False)
            split_all("merged", lambda j, d: do(V_.tensor_copy(d, MERGED[:, j, :]), "tmp_ready"))
            dve.wait_ge(sem("ld_x"), 32)
            for i in range(KT):
                if i == 4:
                    inverse_deviation("mem", M)
                for j in (range(2 * (i - 4), 2 * (i - 4) + 2) if i >= 4 else ()):
                    q = splits["n_mem"][0] + j
                    scaled_by(tmp[:, q % 2, 0:M], MEM[:, j, :], prm("g_mem", j), "tmp_ready", M)
                    if j % 2:
                        low(q - 1)
                        low(q)
                add_to_h(stages["mix_out"][0] + i, i)

            inverse_deviation("x")
            split_all("n_x", lambda j, d: scaled_by(d, H[:, j, :], prm("g_x", j), "tmp_ready"))
            for hd in range(XH):
                dve.wait_ge(sem("x_raw"), hd + 1)
                for c in range(TC):
                    do(V_.tensor_reduce(x_stat[:, c, 0:1], banks[4 + c // 2][:, M * (c % 2):M * (c % 2 + 1)], AX_X,
                                        ALU.max, negate=True), "x_max" if c == TC - 1 else "vector_step")
                dve.wait_ge(sem("x_scored"), hd + 1)
                do(V_.reciprocal(x_stat[:, :, 2:3], x_stat[:, :, 1:2]))
                for c in range(TC):
                    do(V_.tensor_scalar(XP[:, c, :], XP[:, c, :], x_stat[:, c, 2:3], None, ALU.mult),
                       "x_p" if c == TC - 1 else "vector_step")
                dve.wait_ge(sem("x_y"), hd + 1)
                for d in range(2):
                    q = splits["x_o"][0] + 2 * hd + d
                    do(V_.tensor_copy(tmp[:, q % 2, :], banks[6 + d][:]), "tmp_ready")
                for d in range(2):
                    low(splits["x_o"][0] + 2 * hd + d)
            for j in range(KT):
                add_to_h(stages["x_out"][0] + j, j)
            do(V_.memset(spare, 0.0), "x_done")

            inverse_deviation("ffn")
            split_all("n_ffn", lambda j, d: scaled_by(d, H[:, j, :], prm("g_ffn", j), "tmp_ready"))
            dve.wait_ge(sem("c_ready"), 1)

            def modulate(i):
                for u in (ada_units(i) if i < ADA_SPAN else ()):
                    block_, k = divmod(u % ADA, KT)
                    dve.wait_ge(sem(f"ada_landed{u % 4}"), 16 * (u // 4 + 1))
                    if u >= ADA and k == 0:
                        dve.wait_ge(sem("ada_summed"), (u - ADA) // KT + 1)
                    o, w = ADA_SUM[:, UNIT * block_:UNIT * (block_ + 1)], ADA_W[:, u % 4, :]
                    if k == 0:
                        do(V_.tensor_scalar(o, w, c_act[:, k:k + 1], None, ALU.mult), "ada_used")
                    else:
                        do(V_.scalar_tensor_tensor(o, w, c_act[:, k:k + 1], o, ALU.mult, ALU.add), "ada_used")

            for c, _ in enumerate(chunks_of(FF1)):
                t0 = stages[f"up{c}"][0]

                def squared(j, d):
                    evacuated(dve, t0 + j)
                    r = RELU[:, j % 2, :]
                    do(V_.tensor_tensor(d, r, r, ALU.mult), "tmp_ready")
                    modulate(16 * c + j)

                split_all(f"hidden{c}", squared)
                for j in range(KT):
                    add_to_h(stages[f"down{c}"][0] + j, j)
                    modulate(16 * c + 8 + j)
                    if 16 * c + 8 + j == ADA_SPAN + 3:
                        dve.wait_ge(sem("ada_summed"), 2 * ADA // KT)
                        for l in range(LAYERS):
                            do(V_.tensor_tensor(mods[:, ADA * l:ADA * (l + 1)], banks[6][:, ADA * l:ADA * (l + 1)],
                                                prm(f"ada_b{l}", 0, ADA), ALU.add))
                            for i in range(2):
                                do(V_.scalar_tensor_tensor(scaled[:, 16 * l + 8 * i:16 * l + 8 * i + 8],
                                                           mods[:, ADA * l + 24 * i + 8:ADA * l + 24 * i + 16], 1.0,
                                                           prm(f"norm{i + 1}_{l}", 0, 8), ALU.add, ALU.mult))
            inverse_deviation("final")
            for j in range(KT):
                scaled_by(H[:, j, :], H[:, j, :], prm("g_final", j), "final_done")

            for l in range(LAYERS):
                def mod(which, j):
                    return mods[:, ADA * l + 8 * which + j:ADA * l + 8 * which + j + 1]

                def modulated(i):
                    def op(j, d):
                        g = scaled[:, 16 * l + 8 * i + j:16 * l + 8 * i + j + 1]
                        do(V_.scalar_tensor_tensor(d, H[:, j, :], g, banks[4][:], ALU.mult, ALU.mult))
                        do(V_.tensor_scalar(d, d, mod(3 * i, j), None, ALU.add), "tmp_ready")
                    return op

                inverse_deviation(f"n1_{l}")
                split_all(f"n1_{l}", modulated(0))

                def fourier(j, d):
                    dve.wait_ge(sem("f_made"), KT * l + j + 1)
                    do(V_.tensor_copy(d, banks[6 + j % 2][:]), "tmp_ready")

                split_all(f"fourier{l}", fourier)
                gated_pairs(f"fourier_out{l}", True)

                def rotate(hd, what, dst):
                    t0 = stages[f"ret_{what}{l}_{hd}"][0]
                    b0, b1 = banks[t0 % BANKS], banks[(t0 + 1) % BANKS]
                    tile_done(dve, t0 + 1)
                    do(V_.tensor_tensor(ROT[:, 0, :], b0[:], COS, ALU.mult))
                    do(V_.tensor_tensor(ROT[:, 1, :], b1[:], SIN, ALU.mult))
                    do(V_.tensor_tensor(dst[:, 0, :], ROT[:, 0, :], ROT[:, 1, :], ALU.subtract))
                    take_tile(t0, lambda b: V_.tensor_tensor(ROT[:, 0, :], b[:], SIN, ALU.mult))
                    take_tile(t0 + 1, lambda b: V_.tensor_tensor(ROT[:, 1, :], b[:], COS, ALU.mult))
                    do(V_.tensor_tensor(dst[:, 1, :], ROT[:, 0, :], ROT[:, 1, :], ALU.add), "rotated")

                dve.wait_ge(sem("ret_tables"), 32 * (l + 1))
                rotate(0, "q", RQ)
                rotate(0, "k", RKY)
                for hd in range(XH):
                    n = XH * l + hd
                    dve.wait_ge(sem("strip_landed"), 16 * (n + 1))
                    for c in range(TC):
                        dve.wait_ge(sem("ret_raw"), TC * n + c + 1)
                        do(V_.tensor_tensor(RP[:, c, :], banks[4 + c % 2][:], STRIP[:, 384 - P * c:896 - P * c],
                                            ALU.mult), "ret_masked")
                    if hd + 1 < XH:
                        rotate(hd + 1, "q", RQ)
                    dve.wait_ge(sem("ret_mean"), n + 1)
                    for d in range(2):
                        do(V_.scalar_tensor_tensor(RY[:, d, :], banks[6][:], -1.0 / 256, RY[:, d, :], ALU.mult,
                                                   ALU.add), "ret_centred")
                    dve.wait_ge(sem("ret_var"), n + 1)
                    statistic(banks[7][:, 0:TC], 256, TC, EPS)
                    if hd + 1 < XH:
                        rotate(hd + 1, "k", RKY)
                    spread_out()
                    for t in range(*stages[f"ret_g{l}_{hd}"]):
                        evacuated(dve, t)
                    for d in range(2):
                        q = splits[f"ret{l}"][0] + 2 * hd + d
                        do(V_.tensor_tensor(RY[:, d, :], RY[:, d, :], banks[6][:], ALU.mult),
                           "ret_scaled" if d else "vector_step")
                        do(V_.tensor_tensor(tmp[:, q % 2, :], RY[:, d, :], RG[:, d, :], ALU.mult), "tmp_ready")
                    for d in range(2):
                        low(splits[f"ret{l}"][0] + 2 * hd + d)
                gated_pairs(f"ret_out{l}", False)
                split_all(f"m{l}", lambda j, d: do(V_.tensor_copy(d, MERGED[:, j, :]), "tmp_ready"))
                for j in range(KT):
                    add_to_h(stages[f"out{l}"][0] + j, j, mod(2, j))
                inverse_deviation(f"n2_{l}")
                split_all(f"n2_{l}", modulated(1))
                do(V_.memset(FRAW[:, :, 0:8], 0.0))
                do(V_.memset(FRAW[:, :, 520:528], 0.0))
                for c, (a, n_hidden) in enumerate(chunks_of(FF2)):
                    t0 = stages[f"ff_in{l}_{c}"][0]

                    def gated(j, d):
                        i = FF2 * l + a + j
                        for half in range(2):
                            evacuated(dve, t0 + 2 * j + half)
                            raw, o, col = FRAW[:, half, :], CONV[:, i % 2, half, :], FF2 * half + a + j
                            do(V_.tensor_scalar(o, raw[:, 7:7 + S], prm(f"conv0_{l}", col), prm(f"conv_b{l}", col),
                                                ALU.mult, ALU.add))
                            do(V_.scalar_tensor_tensor(o, raw[:, 8:8 + S], prm(f"conv1_{l}", col), o, ALU.mult, ALU.add))
                            do(V_.scalar_tensor_tensor(o, raw[:, 9:9 + S], prm(f"conv2_{l}", col), o, ALU.mult, ALU.add),
                               "conv_done")
                        dve.wait_ge(sem("gelu"), i + 1)
                        do(V_.tensor_tensor(d, CONV[:, i % 2, 0, :], CONV[:, i % 2, 1, :], ALU.mult), "tmp_ready")

                    split_all(f"ff{l}_{c}", gated)
                    for j in range(KT):
                        add_to_h(stages[f"ff_out{l}_{c}"][0] + j, j, mod(5, j))
            inverse_deviation("out")
            for j in range(KT):
                scaled_by(H[:, j, :], H[:, j, :], prm("g_out", j), "y_done")


def constant_arrays():
    f = np.float32
    i = np.arange(P)
    tables = {}
    head, pos = i // CH, i % CH
    same = head[:, None] == head[None, :]
    tables["ident"] = np.eye(P)
    tables["ones"] = np.ones((P, P))
    tables["heads"] = same
    tables["strict"] = same & (pos[:, None] < pos[None, :])
    s = np.arange(CH)
    tables["incl"] = pos[:, None] <= s[None, :]
    levels = [(pos[:, None] // 2 == s[None, :] // 2) & (pos[:, None] < s[None, :])]
    for l in range(1, 6):
        b = 2 ** l
        levels.append((pos[:, None] // (2 * b) == s[None, :] // (2 * b)) & (pos[:, None] % (2 * b) >= b)
                      & (s[None, :] % (2 * b) < b))
    tables["level"] = np.concatenate(levels, 1)
    tables["ident_c"] = pos[:, None] == s[None, :]
    tables["reset"] = np.broadcast_to(np.arange(S) % CH != 0, (P, S))
    table = np.concatenate([np.asarray(tables[n], f) for n, _ in TABLE], 1)

    far = 1e30
    steps = i[:, None] + P - np.arange(2 * P)[None, :]
    dist = [np.where((steps >= 0) & (steps <= P), steps, far)]
    steps = i[:, None] + 3 * P - np.arange(4 * P)[None, :]
    for dilation in (4, 16):
        dist.append(np.where((steps >= 0) & (steps % dilation == 0), steps, far))
    dist = np.concatenate(dist, 1).astype(f)

    a = 2 * np.pi * (np.outer(np.arange(S), np.arange(S)) % S) / S
    dft_cos = (np.cos(a) / np.sqrt(S)).astype(f).reshape(TC, P, S).transpose(1, 0, 2)
    dft_sin = (-np.sin(a) / np.sqrt(S)).astype(f).reshape(TC, P, S).transpose(1, 0, 2)
    a = 2 * np.pi * (np.outer(i, i) % P) / P
    dft_feature = (np.concatenate([np.cos(a), np.sin(a)], 1) / np.sqrt(P)).astype(f)

    inv_freq = (f(10000.0) ** (-i.astype(f) / f(P))).astype(f)
    angle = (inv_freq[:, None] * np.arange(S, dtype=f)[None, :]).astype(f).astype(np.float64)
    rotary = np.stack([np.cos(angle), np.sin(angle)], 1).astype(f)

    strips = []
    d = np.arange(896)[None, :] - 384 - i[:, None]
    for h in range(XH):
        fwd, bwd = np.log1p(-2.0 ** (-5.0 - h)), np.log1p(-2.0 ** (-5.5 - h))
        strips.append(np.exp(np.where(d >= 0, fwd * d, -bwd * d)) / 16)
    return dict(table=table, dist=dist, dft_cos=dft_cos, dft_sin=dft_sin, dft_feature=dft_feature, rotary=rotary,
                strips=np.stack(strips).astype(f))


def feature_major(a):
    return a.T.reshape(-1, P, a.shape[0]).transpose(1, 0, 2)


def pad_to(a, n):
    out = np.zeros(a.shape[:-1] + (n,), a.dtype)
    out[..., :a.shape[-1]] = a
    return out


def lay_out(inputs, plan):
    x = {k: np.asarray(v) for k, v in inputs.items()}
    w_in = x["w_in"]
    names = dict(x)
    names["w_in_lora"] = pad_to(w_in[:, :, 3072:3360], 384)
    order = np.concatenate([np.arange(P) + 1024 * s + P * p for p in range(PAIRS) for s in range(3)])
    names["w_in_pair"] = w_in[:, :, order]
    f = np.float32
    weights = np.zeros((len(plan.source), P, UNIT), f)
    for u, src in enumerate(plan.source):
        if src[0] == "blocks":
            _, name, layer, row, col, k, b0, n = src
            w = names[name][layer]
            for b in range(n):
                j, i = divmod(b0 + b, k)
                weights[u, :, P * b:P * (b + 1)] = w[row + P * i:row + P * (i + 1), col + P * j:col + P * (j + 1)]
        elif src[0] == "rows":
            _, name, layer, row, col, w, per = src
            m = names[name][layer]
            for b in range(per):
                weights[u, :, w * b:w * (b + 1)] = m[row + P * b:row + P * (b + 1), col:col + w]
    ada = x["ada_w_2"].reshape(LAYERS, KT, P, ADA // KT, UNIT).transpose(0, 3, 1, 2, 4).reshape(LAYERS * ADA, P, UNIT)
    w2, a2, g2 = x["w2"][0], x["a2"][0], x["g2"][0]
    lora = np.zeros((PAIRS, P, 4, P), f)
    for p in range(PAIRS):
        c = slice(P * p, P * (p + 1))
        lora[p, 0:64, 0], lora[p, 64:128, 0] = w2[:, c], a2[:, c]
        lora[p, :, 1], lora[p, 0:32, 2] = g2[0:128, c], g2[128:160, c]
    vec = {"g_mix": x["norm_mix_g"], "mu": pad_to(x["shift_mu"], 27 * P), "w0": x["w0"], "a0": x["a0"],
           "k_k": x["k_k"], "k_a": x["k_a"], "r_k": x["r_k"], "gn_w": x["gn_w"], "gn_b": x["gn_b"],
           "g_x": x["norm_x_g"], "g_mem": x["norm_mem_g"], "g_ffn": x["norm_ffn_g"], "g_final": x["norm_final_g"],
           "c": x["c_2"], "g_out": x["final_g_2"]}
    for l in range(LAYERS):
        vec[f"norm1_{l}"], vec[f"norm2_{l}"] = x["norm1_g_2"][l], x["norm2_g_2"][l]
        vec[f"ada_b{l}"], vec[f"conv_b{l}"] = x["ada_b_2"][l], x["conv_b_2"][l]
        for i in range(3):
            vec[f"conv{i}_{l}"] = x["conv_w_2"][l, i]
    params = np.concatenate([vec[n].reshape(-1, P).T for n, _ in PARAMS], 1)
    arrays = dict(weights=weights, ada=ada, lora_w=lora, params=params, x=feature_major(x["x"][0]),
                  mem=feature_major(x["mem"][0]))
    arrays.update(constant_arrays())
    return {k: np.ascontiguousarray(v) for k, v in arrays.items()}


def kernel(**inputs):
    import concourse.bacc as bacc
    from concourse.bass_utils import run_bass_kernel_spmd

    plan = make_plan()
    arrays = lay_out(inputs, plan)
    nc = bacc.Bacc("TRN2", target_bir_lowering=False, num_devices=1, dynamic_dma_scratch_size=1024)
    aps = {k: nc.dram_tensor("in_" + k, a.shape, mybir.dt.from_np(a.dtype), kind="ExternalInput").ap()
           for k, a in arrays.items()}
    out = nc.dram_tensor("out_y", (P, KT, S), F32, kind="ExternalOutput").ap()
    build_program(nc, plan, aps, out)
    r = run_bass_kernel_spmd(nc, [{"in_" + k: a for k, a in arrays.items()}], core_ids=[0])
    y = np.asarray(r.results[0]["out_y"])
    return np.ascontiguousarray(y.transpose(2, 1, 0)).reshape(1, S, D)
```
